# Optimizing a Trainium2 kernel written in Bass

```python
import jax, jax.numpy as jnp
from jax import lax
import numpy as np

D_MODEL = 2048
BATCH = 1
SEQ = 256
DEPTH = 2

HEAD_DIM = 128
POOL_WINDOWS = (2, 4, 8, 16)
N_POOL_GROUPS = len(POOL_WINDOWS)
POOL_WIDTH = D_MODEL // 4
POOL_GROUP = POOL_WIDTH // N_POOL_GROUPS
SCONV_WIDTH = 3 * D_MODEL // 8
CONF_WIDTH = D_MODEL - POOL_WIDTH - SCONV_WIDTH
N_CONF_HEADS = CONF_WIDTH // HEAD_DIM
SCONV_K = 3
CONF_K = 31
IN_PROJ_WIDTH = POOL_WIDTH + 3 * SCONV_WIDTH + 2 * CONF_WIDTH
MIX_WIDTH = POOL_WIDTH + SCONV_WIDTH + CONF_WIDTH

PEER_HEADS = 8
PEER_NKEYS = 128
PEER_EXPERTS = PEER_NKEYS * PEER_NKEYS
PEER_TOPK = 16
PEER_QHALF = 128
PEER_QDIM = 2 * PEER_QHALF
PEER_BLOCK = 128
EPS = 1e-6

kernel_name = "hybrid_pool_shortconv_conformer_peer"

def rmsnorm(x, g):
    x32 = x.astype(jnp.float32)
    y = x32 * lax.rsqrt(jnp.mean(x32 * x32, axis=-1, keepdims=True) + EPS)
    return (y * g.astype(jnp.float32)).astype(x.dtype)

def causal_depthwise_conv(x, w):
    k_width = w.shape[0]
    s = x.shape[1]
    xp = jnp.pad(x, ((0, 0), (k_width - 1, 0), (0, 0)))
    y = xp[:, 0:s] * w[0]
    for k in range(1, k_width):
        y = y + xp[:, k:k + s] * w[k]
    return y

def head_layernorm(x, g, b, n_heads):
    bsz, s, c = x.shape
    x32 = x.astype(jnp.float32).reshape(bsz, s, n_heads, c // n_heads)
    mu = jnp.mean(x32, axis=-1, keepdims=True)
    xc = x32 - mu
    var = jnp.mean(xc * xc, axis=-1, keepdims=True)
    y = (xc * lax.rsqrt(var + EPS)).reshape(bsz, s, c)
    return (y * g.astype(jnp.float32) + b.astype(jnp.float32)).astype(x.dtype)

def pool_mixer(xa, pool_w, pool_scale):
    bsz, s, _ = xa.shape
    x32 = xa.astype(jnp.float32)
    c = jnp.cumsum(x32, axis=1)
    count = jnp.arange(1, s + 1, dtype=jnp.float32)[None, :, None]
    groups = []
    for gi, win in enumerate(POOL_WINDOWS):
        cg = c[..., gi * POOL_GROUP:(gi + 1) * POOL_GROUP]
        prev = jnp.pad(cg, ((0, 0), (win, 0), (0, 0)))[:, :s]
        groups.append((cg - prev) / jnp.minimum(count, float(win)))
    pooled = (jnp.concatenate(groups, axis=-1) - x32).astype(xa.dtype)
    pooled = pooled.reshape(bsz, s, N_POOL_GROUPS, POOL_GROUP)
    y = jnp.einsum('bsgc,gcd->bsgd', pooled, pool_w).reshape(bsz, s, POOL_WIDTH)
    return y * pool_scale

def hybrid_mixer(xn, w_in, pool_w, pool_scale, sconv_w, conf_w, conf_b, conf_ln_g, conf_ln_b, w_out):
    z = xn @ w_in
    o1 = POOL_WIDTH
    o2 = o1 + SCONV_WIDTH
    o3 = o2 + SCONV_WIDTH
    o4 = o3 + SCONV_WIDTH
    o5 = o4 + CONF_WIDTH
    xa = z[..., :o1]
    h_b, gate_b, gate_c = z[..., o1:o2], z[..., o2:o3], z[..., o3:o4]
    conf_val, conf_gate = z[..., o4:o5], z[..., o5:]

    y_a = pool_mixer(xa, pool_w, pool_scale)
    y_b = gate_b * causal_depthwise_conv(gate_c * h_b, sconv_w)
    u = conf_val * jax.nn.sigmoid(conf_gate)
    u = causal_depthwise_conv(u, conf_w) + conf_b
    u = head_layernorm(u, conf_ln_g, conf_ln_b, N_CONF_HEADS)
    y_c = u * jax.nn.sigmoid(u)

    y = jnp.concatenate([y_a, y_b, y_c], axis=-1)
    return y @ w_out

def peer_ffn(xn, wq, k1, k2, u, v):
    bsz, s, d = xn.shape
    t = bsz * s
    xt = xn.reshape(t, d)
    q = (xt @ wq).astype(jnp.float32).reshape(t, PEER_HEADS, 2, PEER_QHALF)
    s1 = jnp.einsum('thc,hnc->thn', q[:, :, 0], k1.astype(jnp.float32))
    s2 = jnp.einsum('thc,hnc->thn', q[:, :, 1], k2.astype(jnp.float32))
    t1, i1 = lax.top_k(s1, PEER_TOPK)
    t2, i2 = lax.top_k(s2, PEER_TOPK)
    cand = (t1[..., :, None] + t2[..., None, :]).reshape(t, PEER_HEADS, PEER_TOPK * PEER_TOPK)
    cidx = (i1[..., :, None] * PEER_NKEYS + i2[..., None, :]).reshape(t, PEER_HEADS, PEER_TOPK * PEER_TOPK)
    top, pos = lax.top_k(cand, PEER_TOPK)
    eidx = jnp.take_along_axis(cidx, pos, axis=-1).reshape(t, PEER_HEADS * PEER_TOPK)
    gate = jax.nn.softmax(top, axis=-1).reshape(t, PEER_HEADS * PEER_TOPK).astype(xn.dtype)

    n_blocks = t // PEER_BLOCK

    def expert_block(args):
        xc, ic, gc = args
        ug = u[ic]
        h = jax.nn.gelu(jnp.einsum('ckd,cd->ck', ug, xc), approximate=False)
        return jnp.einsum('ck,ckd->cd', gc * h, v[ic])

    out = lax.map(expert_block, (xt.reshape(n_blocks, PEER_BLOCK, d),
                                 eidx.reshape(n_blocks, PEER_BLOCK, -1),
                                 gate.reshape(n_blocks, PEER_BLOCK, -1)))
    return out.reshape(bsz, s, d)

def setup_inputs(seed: int = 0) -> dict:
    key = jax.random.key(seed)
    ks = jax.random.split(key, 20)
    f32 = jnp.float32
    L, D = DEPTH, D_MODEL

    def nrm(k, shape, scale):
        return jax.random.normal(k, shape, f32) * scale

    return {
        "x": jax.random.normal(ks[0], (BATCH, SEQ, D), f32),
        "norm1_g": 1.0 + nrm(ks[1], (L, D), 0.05),
        "w_in": nrm(ks[2], (L, D, IN_PROJ_WIDTH), D ** -0.5),
        "pool_w": nrm(ks[3], (L, N_POOL_GROUPS, POOL_GROUP, POOL_GROUP), POOL_GROUP ** -0.5),
        "pool_scale": 1.0 + nrm(ks[4], (L, POOL_WIDTH), 0.1),
        "sconv_w": nrm(ks[5], (L, SCONV_K, SCONV_WIDTH), SCONV_K ** -0.5),
        "conf_w": nrm(ks[6], (L, CONF_K, CONF_WIDTH), CONF_K ** -0.5),
        "conf_b": nrm(ks[7], (L, CONF_WIDTH), 0.02),
        "conf_ln_g": 1.0 + nrm(ks[8], (L, CONF_WIDTH), 0.05),
        "conf_ln_b": nrm(ks[9], (L, CONF_WIDTH), 0.02),
        "w_out": nrm(ks[10], (L, MIX_WIDTH, D), MIX_WIDTH ** -0.5),
        "norm2_g": 1.0 + nrm(ks[11], (L, D), 0.05),
        "peer_wq": nrm(ks[12], (L, D, PEER_HEADS * PEER_QDIM), D ** -0.5),
        "peer_k1": nrm(ks[13], (L, PEER_HEADS, PEER_NKEYS, PEER_QHALF), PEER_QHALF ** -0.5),
        "peer_k2": nrm(ks[14], (L, PEER_HEADS, PEER_NKEYS, PEER_QHALF), PEER_QHALF ** -0.5),
        "peer_u": nrm(ks[15], (L, PEER_EXPERTS, D), D ** -0.5),
        "peer_v": nrm(ks[16], (L, PEER_EXPERTS, D), PEER_HEADS ** -0.5),
        "final_g": 1.0 + nrm(ks[17], (D,), 0.05),
    }

def reference(x, norm1_g, w_in, pool_w, pool_scale, sconv_w, conf_w, conf_b, conf_ln_g, conf_ln_b,
              w_out, norm2_g, peer_wq, peer_k1, peer_k2, peer_u, peer_v, final_g):
    h = x
    for l in range(DEPTH):
        xn = rmsnorm(h, norm1_g[l])
        h = h + hybrid_mixer(xn, w_in[l], pool_w[l], pool_scale[l], sconv_w[l], conf_w[l], conf_b[l],
                             conf_ln_g[l], conf_ln_b[l], w_out[l])
        xn = rmsnorm(h, norm2_g[l])
        h = h + peer_ffn(xn, peer_wq[l], peer_k1[l], peer_k2[l], peer_u[l], peer_v[l])
    return rmsnorm(h, final_g)


_drawn_inputs = setup_inputs


def setup_inputs(seed=0):
    import zlib

    import numpy as np

    out = dict(_drawn_inputs(seed))
    spreads = {}
    factors = {'conf_ln_b': 2.697}
    for name, (base, spread) in spreads.items():
        noise = np.random.default_rng([zlib.crc32(name.encode()), seed]).standard_normal(out[name].shape)
        drawn = base * np.exp(spread * noise) if base else spread * noise
        out[name] = __import__('jax').numpy.asarray(drawn.astype(out[name].dtype))
    for name, factor in factors.items():
        out[name] = (out[name] * factor).astype(out[name].dtype)
    return out
```

```python
import numpy as np
import concourse.bass as bass
from concourse import mybir
from contextlib import ExitStack

F32 = mybir.dt.float32
F32R = mybir.dt.float32r
U32 = mybir.dt.uint32
ACT = mybir.ActivationFunctionType
ALU = mybir.AluOpType
AX = mybir.AxisListType

P = 128
T = 256
D = 2048
LAYERS = 2
TT = T // P
KT = D // P
POOL_TILES, SCONV_TILES, CONF_TILES = 4, 6, 6
SCONV_K, CONF_K = 3, 31
WINDOWS = (2, 4, 8, 16)
HEADS, TOPK, KEYS = 8, 16, 128
PICKS = HEADS * TOPK
EPS = 1e-6
NEG = -3.0e38

WIN_ORDER = (list(range(4)) + [n for i in range(6) for n in (22 + i, 28 + i)]
             + list(range(4, 10)) + list(range(16, 22)) + list(range(10, 16)))

G_IN, G_OUT, G_Q, G_U, G_V = 17, 8, 8, 64, 64
AT_IN = 0
AT_OUT = AT_IN + G_IN
AT_Q = AT_OUT + G_OUT
AT_U = AT_Q + G_Q
AT_V = AT_U + G_U
G_LAYER = AT_V + G_V
P1_IN, P1_Q, P1_U, P1_LAYER = 0, G_IN, G_IN + G_Q, G_IN + G_Q + G_U
P2_OUT, P2_V, P2_LAYER = 0, G_OUT, G_OUT + G_V

C_G1, C_G2 = 0, 16
C_PS = 32
C_SW = C_PS + POOL_TILES
C_CW = C_SW + SCONV_K * SCONV_TILES
C_CB = C_CW + CONF_TILES * CONF_K
C_LG = C_CB + CONF_TILES
C_LB = C_LG + CONF_TILES
C_PW = C_LB + CONF_TILES
N_PAR = C_PW + POOL_TILES * P

W_TILES = 128
Y0 = 0
XN0 = 16
Z0 = 32
ZC0 = Z0 + 4
ZH0, ZGC0, ZGB0 = Z0 + 16, Z0 + 22, Z0 + 28
PPAD0, XPAD0, SA0, SB0 = 66, 73, 78, 83
U0, ACC0, C0, XC0, SQ0, SACC0, INV0, LNY0 = 88, 90, 92, 98, 104, 110, 116, 120
JUNK0 = 98
KEY0, QT0, S0 = 0, 8, 112
PP, XP, UP = SCONV_K - 1 + T + 2, 16 + T, 32 + T

TOPK_BODIES = TT * HEADS
U_TOPK0 = 1
U_GATES = 40
U_GATES_SUM = 43
U_PICKS = 46
CREDIT = 8


def build(nc, x, win, wout, wq, ut, vt, params, keys, final_g, iota, ident, invcnt, out):
    hs = nc.dram_tensor("h_saved_rows", (P, TT, D), F32, kind="Internal").ap()
    ctx = ExitStack()
    with ctx:
        cursor = [(nc.sbuf_base + 63) // 64 * 64]

        def region(nbytes):
            at = cursor[0]
            cursor[0] += (nbytes + 31) // 32 * 32
            return at

        def sb(name, shape, dt, at=None):
            nbytes = 4 * int(np.prod(shape[1:]))
            return nc.alloc_sbuf_tensor_at(name, shape, dt, offset=region(nbytes) if at is None else at)

        def sem(name):
            return ctx.enter_context(nc.semaphore(name))

        W = sb("W", [P, W_TILES, T], F32)
        at_xa, at_xb = region(16384), region(16384)
        Xhi = sb("Xhi", [P, KT, T], F32R, at_xa)
        Xlo = sb("Xlo", [P, KT, T], F32R, at_xb)
        H = sb("H", [P, TT, D], F32, at_xa)
        Yhi = sb("Yhi", [P, 2, T], F32R, at_xb)
        Ylo = sb("Ylo", [P, 2, T], F32R, at_xb + 2048)
        OneA = sb("OneA", [P, 2, 4, P], F32, at_xb + 4096)
        OneB = sb("OneB", [P, 2, 4, P], F32, at_xb + 8192)
        FG = sb("FG", [P, D], F32, at_xb)
        RAW = sb("RAW", [P, 4, 1024], F32)
        HI = sb("HI", [P, 4, 512], F32R)
        LO = sb("LO", [P, 4, 512], F32R)
        PAR = sb("PAR", [P, N_PAR], F32)
        IOTA = sb("IOTA", [P, P], F32)
        IDENT = sb("IDENT", [P, P], F32)
        ONES = sb("ONES", [P, P], F32)
        at_top = region(4096)
        CAND = sb("CAND", [P, 256], F32, at_top)
        CAND2 = sb("CAND2", [P, 256], F32, at_top + 1024)
        EQ1 = sb("EQ1", [P, TOPK, TOPK], F32, at_top + 2048)
        EQ2 = sb("EQ2", [P, TOPK, TOPK], F32, at_top + 3072)
        PT = sb("PT", [P, 3, T], F32, at_top)
        SC = sb("SC", [P, 2, KEYS], F32)
        SC2 = sb("SC2", [P, 2, KEYS], F32)
        TV = sb("TV", [P, 2, TOPK], F32)
        TI = sb("TI", [P, 2, TOPK], U32)
        TIF = sb("TIF", [P, 2, TOPK], F32)
        BV = sb("BV", [P, TOPK], F32)
        BI = sb("BI", [P, TOPK], U32)
        BAB = sb("BAB", [P, 2, TOPK], U32)
        PK = sb("PK", [P, 3, TT, PICKS], F32)
        SUMS = sb("SUMS", [P, TT * HEADS], F32)
        STAT = sb("STAT", [P, 8, TT], F32)
        WC = sb("WC", [P, CONF_K + 1], F32)
        PS = sb("PS", [P, 3, 8], F32)
        assert cursor[0] <= nc.sbuf_usable_end, (cursor[0], nc.sbuf_usable_end)
        bank = [ctx.enter_context(nc.psum_tensor(f"bank{i}", [P, 512], F32)) for i in range(8)]

        def tiles(first, n):
            return W[:, first:first + n, :]

        def flat(first, n):
            return W[:, first:first + n, :].rearrange("p a t -> p (a t)")

        XN = flat(XN0, 16).rearrange("p (a d) -> p a d", a=TT)
        PPAD = flat(PPAD0, 7)[:, 0:SCONV_TILES * PP].rearrange("p (a t) -> p a t", t=PP)
        XPAD = flat(XPAD0, 5)[:, 0:POOL_TILES * XP].rearrange("p (a t) -> p a t", t=XP)
        SA = flat(SA0, 5)[:, 0:POOL_TILES * XP].rearrange("p (a t) -> p a t", t=XP)
        SB = flat(SB0, 5)[:, 0:POOL_TILES * XP].rearrange("p (a t) -> p a t", t=XP)
        UPAD = flat(U0, 2)[:, 0:UP]
        KEY = flat(KEY0, 8).rearrange("p (j n) -> p j n", n=KEYS)
        SBUFQ = flat(S0, 16).rearrange("p (a j n) -> p a j n", a=TT, n=KEYS)

        def pool_out(n):
            return bank[6 + n // 2][:, (n % 2) * T:(n % 2 + 1) * T]

        const_in = sem("const_in")
        x_in = sem("x_in")
        final_in = sem("final_in")
        par_in = sem("par_in")
        inv_in = sem("inv_in")
        keys_in = sem("keys_in")
        raw_in = [sem(f"raw_in{s}") for s in range(4)]
        hi_done = sem("hi_done")
        lo_done = sem("lo_done")
        mm_done = sem("mm_done")
        evac_done = sem("evac_done")
        yhi_done = sem("yhi_done")
        ylo_done = sem("ylo_done")
        h_ready = sem("h_ready")
        h_saved = sem("h_saved")
        h_back = sem("h_back")
        ssq_done = sem("ssq_done")
        var_done = sem("var_done")
        std_done = sem("std_done")
        rstd_done = sem("rstd_done")
        xn_act = sem("xn_act")
        xn_dve = sem("xn_dve")
        tr_done = sem("tr_done")
        xhi_done = sem("xhi_done")
        xlo_done = sem("xlo_done")
        pool_rows = sem("pool_rows")
        pool_mm = sem("pool_mm")
        pool_used = sem("pool_used")
        conf_rows = sem("conf_rows")
        mean_mm = sem("mean_mm")
        cent_done = sem("cent_done")
        sq_done = sem("sq_done")
        var_mm = sem("var_mm")
        lstd_done = sem("lstd_done")
        lny_done = sem("lny_done")
        sig_done = sem("sig_done")
        mixed = sem("mixed")
        s_mm = sem("s_mm")
        s_out = sem("s_out")
        topk_done = sem("topk_done")
        exp_done = sem("exp_done")
        gates_done = sem("gates_done")
        pt_mm = sem("pt_mm")
        picks_done = sem("picks_done")
        hot_done = sem("hot_done")
        g_mm = sem("g_mm")
        g_used = sem("g_used")
        gated = sem("gated")
        passed = sem("passed")
        out_ready = sem("out_ready")
        out_done = sem("out_done")

        block = ctx.enter_context(nc.Block())

        def stand(eng, semaphore, value):
            eng.wait_ge(semaphore, value)
            eng.sem_inc(passed, 1)

        def G(layer, phase, i):
            return layer * G_LAYER + phase + i

        @block.sync
        def _(sp):
            def load(layer, src, per_layer, phase, n_groups):
                with sp.Fori(0, n_groups) as i:
                    for s in range(4):
                        sp.wait_ge(lo_done, G(layer, phase, i) * 8 + 2 * s + 2)
                        sp.dma_start(
                            RAW[:, s, :],
                            src[bass.ds(layer * per_layer + i * 2 + s // 2, 1), :,
                                (s % 2) * 1024:(s % 2 + 1) * 1024].rearrange("a p n -> p (a n)"),
                        ).then_inc(raw_in[s], 16)

            with sp.Fori(0, LAYERS) as layer:
                load(layer, win, 2 * G_IN, AT_IN, G_IN)
                load(layer, wout, 2 * G_OUT, AT_OUT, G_OUT)
                load(layer, wq, 2 * G_Q, AT_Q, G_Q)
                load(layer, ut, 2 * G_U, AT_U, G_U)
                load(layer, vt, 2 * G_V, AT_V, G_V)
            for a in range(TT):
                sp.wait_ge(out_ready, a + 1)
                sp.dma_start(out[0, a * P:(a + 1) * P, :], H[:, a, :]).then_inc(out_done, 16)
            sp.wait_ge(out_done, 16 * TT)

        @block.gpsimd
        def _(pool):
            pool.dma_start(IOTA[:, :], iota).then_inc(const_in, 16)
            pool.dma_start(IDENT[:, :], ident).then_inc(const_in, 16)

            def save(norm):
                stand(pool, h_ready, norm + 1)
                pool.dma_start(hs, H[:, :, :]).then_inc(h_saved, 16)

            def bring_back(norm, first_group):
                stand(pool, mm_done, first_group * 8 + CREDIT)
                stand(pool, h_saved, norm * 16 + 16)
                pool.dma_start(H[:, :, :], hs).then_inc(h_back, 16)

            with pool.Fori(0, LAYERS) as layer:
                stand(pool, h_ready, layer * 2 + 1)
                pool.dma_start(PAR[:, :], params[bass.ds(layer, 1), :, :].rearrange("a p n -> p (a n)")).then_inc(par_in, 16)
                save(layer * 2)
                pool.dma_start(flat(INV0, 4), invcnt).then_inc(inv_in, 16)
                bring_back(layer * 2, G(layer, AT_OUT, 0))
                save(layer * 2 + 1)
                pool.dma_start(flat(KEY0, 8), keys[bass.ds(layer, 1), :, :].rearrange("a p n -> p (a n)")).then_inc(keys_in, 16)
                bring_back(layer * 2 + 1, G(layer, AT_V, 0))
            stand(pool, h_ready, 2 * LAYERS + 1)
            pool.dma_start(FG[:, :], final_g.unsqueeze(0).to_broadcast([P, D])).then_inc(final_in, 16)

        @block.scalar
        def _(act):
            act.dma_start(H[:, :, :], x.rearrange("(a p) d -> p a d", p=P)).then_inc(x_in, 16)

            def hi(g, q):
                if q % 2 == 0:
                    act.wait_ge(raw_in[q // 2], g * 16 + 16)
                act.wait_ge(mm_done, g * 8 + q + 5)
                nc.scalar.activation(HI[:, q % 4, :], RAW[:, q // 2, (q % 2) * 512:(q % 2 + 1) * 512],
                                     ACT.Copy).then_inc(hi_done, 1)

            def evac(g, t, dst, func):
                act.wait_ge(mm_done, g * 8 + 4 * t + 4 + CREDIT)
                nc.scalar.activation(dst, bank[t][:, 0:T], func).then_inc(evac_done, 1)

            def p1_group(g, before, after):
                for q in range(4):
                    hi(g, q)
                if before:
                    before()
                for q in range(4, 8):
                    hi(g, q)
                after()

            def wtile(n):
                return W[:, bass.ds(n, 1), :].rearrange("p a t -> p (a t)")

            def norm(number, gain, par_value):
                act.wait_ge(h_ready, number + 1)
                nc.scalar.activation(flat(JUNK0, 8), H[:, 0, :], ACT.Square,
                                     accum_out=STAT[:, 0, 0:1]).then_inc(ssq_done, 1)
                act.wait_ge(var_done, number + 1)
                nc.scalar.activation(STAT[:, 2, :], STAT[:, 1, :], ACT.Sqrt).then_inc(std_done, 1)
                if gain is None:
                    return
                act.wait_ge(rstd_done, number + 1)
                for c in range(2):
                    nc.scalar.activation(XN[:, 1, c * 1024:(c + 1) * 1024], H[:, 1, c * 1024:(c + 1) * 1024],
                                         ACT.Copy, scale=STAT[:, 3, 1:2]).then_inc(xn_act, 1)
                act.wait_ge(h_saved, number * 16 + 16)
                act.wait_ge(xn_dve, number * 2 + 2)
                act.wait_ge(xn_act, number * 2 + 2)
                act.wait_ge(par_in, par_value)
                for k in range(KT):
                    act.wait_ge(tr_done, number * KT + k + 1)
                    nc.scalar.activation(Xhi[:, k, :], bank[k % 8][:, 0:T],
                                         ACT.Copy, scale=PAR[:, gain + k:gain + k + 1]).then_inc(xhi_done, 1)

            def combine(layer, phase, p2_base, n_groups, ready, ready_value):
                act.wait_ge(ready, ready_value)
                with act.Fori(0, n_groups) as i:
                    g = G(layer, phase, i)
                    for t in range(2):
                        act.wait_ge(mm_done, g * 8 + 4 * t + 4)
                        nc.scalar.activation(Yhi[:, t, :], wtile(i * 2 + t), ACT.Copy).then_inc(yhi_done, 1)
                        for q in range(4 * t, 4 * t + 4):
                            hi(g, q)

            with act.Fori(0, LAYERS) as layer:
                norm(layer * 2, C_G1, layer * 16 + 16)

                act.preload_act_table(ACT.Sigmoid)

                def z(i, t):
                    return wtile(i * 2 + (Z0 + t))

                def in_group(i, prev_func):
                    g = G(layer, AT_IN, i)
                    before = None
                    if prev_func is not None:
                        def before():
                            evac(g - 1, 1, z(i, -1), prev_func)
                    p1_group(g, before, lambda: evac(g, 0, z(i, 0), ACT.Copy))

                in_group(0, None)
                with act.Fori(1, 3) as i:
                    in_group(i, ACT.Copy)
                with act.Fori(3, 9) as i:
                    in_group(i, ACT.Sigmoid)
                with act.Fori(9, G_IN) as i:
                    in_group(i, ACT.Copy)
                evac(G(layer, AT_IN, G_IN - 1), 1, W[:, Z0 + 2 * G_IN - 1, :], ACT.Copy)

                for c in range(3):
                    act.wait_ge(cent_done, layer * 3 + c + 1)
                    nc.scalar.activation(flat(SQ0 + 2 * c, 2), flat(XC0 + 2 * c, 2), ACT.Square).then_inc(sq_done, 1)
                act.preload_act_table(ACT.Sqrt)
                for c in range(3):
                    act.wait_ge(var_mm, layer * 3 + c + 1)
                    nc.scalar.activation(flat(SQ0 + 2 * c, 2), bank[5 + c][:, :], ACT.Sqrt, bias=EPS).then_inc(lstd_done, 1)
                act.preload_act_table(ACT.Sigmoid)
                for c in range(3):
                    act.wait_ge(lny_done, layer * 3 + c + 1)
                    nc.scalar.activation(flat(XC0 + 2 * c, 2), flat(LNY0 + 2 * c, 2), ACT.Sigmoid).then_inc(sig_done, 1)

                combine(layer, AT_OUT, P2_OUT, G_OUT, mixed, layer + 1)
                norm(layer * 2 + 1, C_G2, layer * 16 + 16)

                act.preload_act_table(ACT.Gelu)

                def evac_q(i, t):
                    if t == 0:
                        act.wait_ge(s_mm, layer * HEADS + i)
                    evac(G(layer, AT_Q, i), t, W[:, QT0 + t, :], ACT.Copy)

                p1_group(G(layer, AT_Q, 0), None, lambda: evac(G(layer, AT_Q, 0), 0, W[:, QT0, :], ACT.Copy))
                with act.Fori(1, G_Q) as i:
                    p1_group(G(layer, AT_Q, i), lambda: evac_q(i - 1, 1), lambda: evac_q(i, 0))

                def u_group(i, before):
                    g = G(layer, AT_U, i)
                    p1_group(g, before, lambda: evac(g, 0, wtile(i * 2), ACT.Gelu))

                def u_before(i):
                    return lambda: evac(G(layer, AT_U, i) - 1, 1, wtile(i * 2 - 1), ACT.Gelu)

                u_group(0, lambda: evac_q(G_Q - 1, 1))
                with act.Fori(1, U_GATES) as i:
                    u_group(i, u_before(i))
                act.wait_ge(topk_done, layer + 1)
                gate_logits = PK[:, 0, :, :].rearrange("p a k -> p (a k)")
                nc.scalar.activation(gate_logits, gate_logits, ACT.Exp).then_inc(exp_done, 1)
                act.preload_act_table(ACT.Gelu)
                with act.Fori(U_GATES, G_U) as i:
                    u_group(i, u_before(i))
                evac(G(layer, AT_U, G_U - 1), 1, W[:, W_TILES - 1, :], ACT.Gelu)

                combine(layer, AT_V, P2_V, G_V, gated, layer + 1)

            norm(2 * LAYERS, None, None)

        @block.vector
        def _(dve):
            tt = nc.vector.tensor_tensor
            ts = nc.vector.tensor_scalar
            stt = nc.vector.scalar_tensor_tensor

            def lo(g, q):
                dve.wait_ge(hi_done, g * 8 + q + 1)
                tt(LO[:, q % 4, :], RAW[:, q // 2, (q % 2) * 512:(q % 2 + 1) * 512],
                   HI[:, q % 4, :].bitcast(F32), ALU.subtract).then_inc(lo_done, 1)

            def lo_group(g, side=None):
                for q in range(8):
                    lo(g, q)
                    if side:
                        side(q)

            def plain(layer, phase, first, end):
                with dve.Fori(first, end) as i:
                    lo_group(G(layer, phase, i))

            def norm(number, gain, par_value):
                dve.wait_ge(h_ready, number + 1)
                nc.vector.tensor_tensor_reduce(out=XN[:, 0, :], in0=H[:, 1, :], in1=H[:, 1, :], scale=1.0,
                                               scalar=0.0, op0=ALU.mult, op1=ALU.add, accum_out=STAT[:, 0, 1:2])
                dve.drain()
                dve.wait_ge(ssq_done, number + 1)
                ts(STAT[:, 1, :], STAT[:, 0, :], 1.0 / D, EPS, ALU.mult, ALU.add).then_inc(var_done, 1)
                dve.wait_ge(std_done, number + 1)
                nc.vector.reciprocal(STAT[:, 3, :], STAT[:, 2, :])
                dve.drain()
                tt(STAT[:, 4, :], STAT[:, 3, :], STAT[:, 3, :], ALU.mult)
                dve.drain()
                tt(STAT[:, 5, :], STAT[:, 4, :], STAT[:, 1, :], ALU.mult)
                dve.drain()
                ts(STAT[:, 6, :], STAT[:, 5, :], -0.5, 1.5, ALU.mult, ALU.add)
                dve.drain()
                tt(STAT[:, 3, :], STAT[:, 3, :], STAT[:, 6, :], ALU.mult).then_inc(rstd_done, 1)
                dve.drain()
                if gain is None:
                    return
                for c in range(2):
                    ts(XN[:, 0, c * 1024:(c + 1) * 1024], H[:, 0, c * 1024:(c + 1) * 1024],
                       STAT[:, 3, 0:1], None, ALU.mult).then_inc(xn_dve, 1)
                dve.wait_ge(par_in, par_value)
                for k in range(KT):
                    dve.wait_ge(xhi_done, number * KT + k + 1)
                    stt(Xlo[:, k, :], bank[k % 8][:, 0:T],
                        PAR[:, gain + k:gain + k + 1], Xhi[:, k, :].bitcast(F32),
                        ALU.mult, ALU.subtract).then_inc(xlo_done, 1)

            def combine(layer, phase, p2_base, n_groups, back):
                with dve.Fori(0, n_groups) as i:
                    g = G(layer, phase, i)
                    for t in range(2):
                        dve.wait_ge(yhi_done, layer * (2 * P2_LAYER) + i * 2 + (2 * p2_base + t + 1))
                        tt(Ylo[:, t, :], W[:, bass.ds(i * 2 + t, 1), :].rearrange("p a t -> p (a t)"),
                           Yhi[:, t, :].bitcast(F32), ALU.subtract).then_inc(ylo_done, 1)
                        for q in range(4 * t, 4 * t + 4):
                            lo(g, q)
                dve.wait_ge(mm_done, G(layer, phase, n_groups) * 8 + CREDIT)
                dve.wait_ge(h_back, back * 16 + 16)
                for a in range(TT):
                    for c in range(4):
                        rows = H[:, a, c * 512:(c + 1) * 512]
                        last = tt(rows, bank[a * 4 + c][:, :], rows, ALU.add)
                dve.drain().then_inc(h_ready, 1)

            dve.sem_inc(lo_done, CREDIT)
            dve.sem_inc(evac_done, 2)
            dve.sem_inc(g_used, 2)
            dve.sem_inc(s_out, 1)
            nc.vector.memset(ONES[:, :], 1.0 / P)
            dve.wait_ge(x_in, 16)
            dve.sem_inc(h_ready, 1)
            dve.wait_ge(const_in, 32)

            with dve.Fori(0, LAYERS) as layer:
                norm(layer * 2, C_G1, layer * 16 + 16)

                def z_done(n):
                    return layer * (2 * P1_LAYER) + n + 1 + 2

                nc.vector.memset(PPAD[:, :, 0:SCONV_K - 1], 0.0)
                nc.vector.memset(XPAD[:, :, 0:16], 0.0)
                nc.vector.memset(SA[:, :, 0:16], 0.0)
                nc.vector.memset(SB[:, :, 0:16], 0.0)
                nc.vector.memset(UPAD[:, 0:32], 0.0)
                plain(layer, AT_IN, 0, 3)

                dve.wait_ge(evac_done, z_done(3))
                dve.wait_ge(inv_in, layer * 16 + 16)
                nc.vector.tensor_copy(XPAD[:, :, 16:XP], tiles(Z0, 4))
                dve.drain()
                steps = [(XPAD, SA, 0, 1), (SA, SB, 1, 2), (SB, SA, 2, 4), (SA, SB, 3, 8)]
                for src, dst, first, shift in steps:
                    tt(dst[:, first:4, 16:XP], src[:, first:4, 16:XP], src[:, first:4, 16 - shift:XP - shift], ALU.add)
                    dve.drain()
                    tt(tiles(SACC0 + first, 1).rearrange("p a t -> p (a t)"), dst[:, first, 16:XP],
                       W[:, INV0 + first, :], ALU.mult)
                    dve.drain()
                tt(tiles(LNY0, 4), tiles(SACC0, 4), tiles(Z0, 4), ALU.subtract).then_inc(pool_rows, 1)

                lo_group(G(layer, AT_IN, 3))

                with dve.Fori(0, CONF_TILES) as j:
                    accs = [W[:, ACC0, :], W[:, ACC0 + 1, :]]

                    def taps(pair):
                        for k in (2 * pair, 2 * pair + 1):
                            if k >= CONF_K:
                                continue
                            src, acc = UPAD[:, 2 + k:2 + k + T], accs[k % 2]
                            if k == 0:
                                ts(acc, src, WC[:, 0:1], WC[:, CONF_K:CONF_K + 1], ALU.mult, ALU.add)
                            elif k == 1:
                                ts(acc, src, WC[:, 1:2], None, ALU.mult)
                            else:
                                stt(acc, src, WC[:, k:k + 1], acc, ALU.mult, ALU.add)
                        dve.drain()

                    def first_side(q):
                        if q == 0:
                            dve.wait_ge(evac_done, layer * (2 * P1_LAYER) + j * 2 + (4 + 2 + 2))
                            pair = W[:, bass.ds(j * 2 + ZC0, 2), :]
                            tt(UPAD[:, 32:UP], pair[:, 0, :], pair[:, 1, :], ALU.mult)
                            nc.vector.tensor_copy(WC[:, 0:CONF_K], PAR[:, bass.ds(j * CONF_K + C_CW, CONF_K)])
                            nc.vector.tensor_copy(WC[:, CONF_K:CONF_K + 1], PAR[:, bass.ds(j + C_CB, 1)])
                            dve.drain()
                        taps(q)

                    def second_side(q):
                        taps(8 + q)
                        if q == 7:
                            tt(W[:, bass.ds(j + C0, 1), :].rearrange("p a t -> p (a t)"), accs[0], accs[1],
                               ALU.add).then_inc(conf_rows, 1)
                            dve.drain()

                    lo_group(G(layer, AT_IN, j * 2 + 4), first_side)
                    lo_group(G(layer, AT_IN, j * 2 + 5), second_side)
                lo_group(G(layer, AT_IN, G_IN - 1))

                dve.wait_ge(pool_mm, layer + 1)
                for n in range(POOL_TILES):
                    last = ts(W[:, Y0 + n, :], pool_out(n), PAR[:, C_PS + n:C_PS + n + 1], None, ALU.mult)
                last.then_inc(pool_used, 1)

                for c in range(3):
                    dve.wait_ge(mean_mm, layer * 3 + c + 1)
                    tt(flat(XC0 + 2 * c, 2), flat(C0 + 2 * c, 2), bank[2 + c][:, :], ALU.subtract).then_inc(cent_done, 1)
                dve.wait_ge(evac_done, z_done(2 * G_IN - 1))
                tt(PPAD[:, :, 2:2 + T], tiles(ZGC0, 6), tiles(ZH0, 6), ALU.mult)
                dve.drain()
                for k in range(SCONV_K):
                    for n in range(SCONV_TILES):
                        w = PAR[:, C_SW + k * SCONV_TILES + n:C_SW + k * SCONV_TILES + n + 1]
                        acc, src = W[:, SACC0 + n, :], PPAD[:, n, k:k + T]
                        if k == 0:
                            ts(acc, src, w, None, ALU.mult)
                        else:
                            stt(acc, src, w, acc, ALU.mult, ALU.add)
                    dve.drain()
                tt(tiles(Y0 + POOL_TILES, 6), tiles(SACC0, 6), tiles(ZGB0, 6), ALU.mult)
                for c in range(3):
                    dve.wait_ge(lstd_done, layer * 3 + c + 1)
                    nc.vector.reciprocal(flat(C0 + 2 * c, 2), flat(SQ0 + 2 * c, 2))
                    dve.drain()
                    tt(flat(XC0 + 2 * c, 2), flat(XC0 + 2 * c, 2), flat(C0 + 2 * c, 2), ALU.mult)
                    dve.drain()
                    for n in (2 * c, 2 * c + 1):
                        last = ts(W[:, LNY0 + n, :], W[:, XC0 + n, :], PAR[:, C_LG + n:C_LG + n + 1],
                                  PAR[:, C_LB + n:C_LB + n + 1], ALU.mult, ALU.add)
                    dve.drain().then_inc(lny_done, 1)
                for c in range(3):
                    dve.wait_ge(sig_done, layer * 3 + c + 1)
                    tt(flat(Y0 + 10 + 2 * c, 2), flat(LNY0 + 2 * c, 2), flat(XC0 + 2 * c, 2), ALU.mult)
                dve.drain().then_inc(mixed, 1)
                combine(layer, AT_OUT, P2_OUT, G_OUT, layer * 2)
                norm(layer * 2 + 1, C_G2, layer * 16 + 16)

                def scores_out(head, count):
                    dve.wait_ge(s_mm, count)
                    nc.vector.tensor_copy(SBUFQ[:, :, bass.ds(head * 2, 2), :],
                                          bank[2][:, :].rearrange("p (a j n) -> p a j n", a=TT, n=KEYS)
                                          ).then_inc(s_out, 1)

                lo_group(G(layer, AT_Q, 0))
                with dve.Fori(1, G_Q) as i:
                    lo_group(G(layer, AT_Q, i))
                    scores_out(i - 1, layer * HEADS + i)
                lo_group(G(layer, AT_U, 0))
                scores_out(HEADS - 1, layer * HEADS + HEADS)
                dve.drain()

                with dve.Fori(0, TOPK_BODIES) as b:
                    def half_topk(h):
                        first, second = slice(0, 8), slice(8, 16)
                        nc.vector.max(TV[:, h, first], SC[:, h, :])
                        dve.drain()
                        nc.vector.max_index(TI[:, h, first], TV[:, h, first], SC[:, h, :])
                        nc.vector.match_replace(SC2[:, h, :], TV[:, h, first], SC[:, h, :], NEG)
                        dve.drain()
                        nc.vector.max(TV[:, h, second], SC2[:, h, :])
                        dve.drain()
                        nc.vector.max_index(TI[:, h, second], TV[:, h, second], SC2[:, h, :])

                    def side_a(q):
                        if q == 0:
                            nc.vector.tensor_copy(
                                SC[:, :, :],
                                flat(S0, 16)[:, bass.ds(b * (2 * KEYS), 2 * KEYS)].rearrange("p (j n) -> p j n", n=KEYS))
                            dve.drain()
                        elif q == 2:
                            half_topk(0)
                        elif q == 4:
                            half_topk(1)
                        elif q == 6:
                            dve.drain()
                            nc.vector.tensor_copy(TIF[:, :, :], TI[:, :, :])
                            tt(CAND[:, :].rearrange("p (a b) -> p a b", b=TOPK),
                               TV[:, 0, :].unsqueeze(2).to_broadcast([P, TOPK, TOPK]),
                               TV[:, 1, :].unsqueeze(1).to_broadcast([P, TOPK, TOPK]), ALU.add)
                            dve.drain()

                    def chosen(h, eq):
                        tt(eq[:, :, :], BAB[:, h, :].unsqueeze(2).to_broadcast([P, TOPK, TOPK]),
                           IOTA[:, 0:TOPK].unsqueeze(1).to_broadcast([P, TOPK, TOPK]), ALU.is_equal)

                    def times_keys(h, eq):
                        tt(eq[:, :, :], eq[:, :, :], TIF[:, h, :].unsqueeze(1).to_broadcast([P, TOPK, TOPK]), ALU.mult)

                    def summed(h, eq):
                        nc.vector.tensor_reduce(
                            PK[:, 1 + h, :, :].rearrange("p a k -> p (a k)")[:, bass.ds(b * TOPK, TOPK)],
                            eq[:, :, :], AX.X, ALU.add)

                    def side_b(q):
                        if q == 0:
                            nc.vector.max(BV[:, 0:8], CAND[:, :])
                            dve.drain()
                            nc.vector.max_index(BI[:, 0:8], BV[:, 0:8], CAND[:, :])
                            nc.vector.match_replace(CAND2[:, :], BV[:, 0:8], CAND[:, :], NEG)
                            dve.drain()
                        elif q == 1:
                            nc.vector.max(BV[:, 8:16], CAND2[:, :])
                            dve.drain()
                            nc.vector.max_index(BI[:, 8:16], BV[:, 8:16], CAND2[:, :])
                            dve.drain()
                        elif q == 2:
                            ts(BAB[:, 0, :], BI[:, :], 4, None, ALU.logical_shift_right)
                            ts(BAB[:, 1, :], BI[:, :], 15, None, ALU.bitwise_and)
                            ts(PK[:, 0, :, :].rearrange("p a k -> p (a k)")[:, bass.ds(b * TOPK, TOPK)],
                               BV[:, :], BV[:, 0:1], None, ALU.subtract)
                            dve.drain()
                        elif q == 3:
                            chosen(0, EQ1)
                            chosen(1, EQ2)
                            dve.drain()
                        elif q == 5:
                            times_keys(0, EQ1)
                            times_keys(1, EQ2)
                            dve.drain()
                        elif q == 6:
                            summed(0, EQ1)
                            summed(1, EQ2)
                            dve.drain()

                    lo_group(G(layer, AT_U, b * 2 + U_TOPK0), side_a)
                    lo_group(G(layer, AT_U, b * 2 + U_TOPK0 + 1), side_b)
                dve.drain().then_inc(topk_done, 1)
                plain(layer, AT_U, U_TOPK0 + 2 * TOPK_BODIES, U_GATES_SUM)

                dve.wait_ge(exp_done, layer + 1)
                by_head = PK[:, 0, :, :].rearrange("p a (h k) -> p (a h) k", k=TOPK)
                nc.vector.tensor_reduce(SUMS[:, :], by_head, AX.X, ALU.add)
                dve.drain()
                nc.vector.reciprocal(SUMS[:, :], SUMS[:, :])
                dve.drain()
                tt(by_head, by_head, SUMS[:, :].unsqueeze(2).to_broadcast([P, TT * HEADS, TOPK]), ALU.mult).then_inc(gates_done, 1)
                plain(layer, AT_U, U_GATES_SUM, U_PICKS)
                for n in range(3):
                    dve.wait_ge(pt_mm, layer * 3 + n + 1)
                    nc.vector.tensor_copy(PT[:, n, :], bank[2 + n][:, 0:T])
                dve.drain().then_inc(picks_done, 1)
                plain(layer, AT_U, U_PICKS, G_U)

                def hot(slot):
                    tt(OneB[:, slot, :, :], IOTA[:, :].unsqueeze(1).to_broadcast([P, 4, P]),
                       PS[:, 2, slot * 4:slot * 4 + 4].unsqueeze(2).to_broadcast([P, 4, P]), ALU.is_equal)
                    for j in range(4):
                        c = slot * 4 + j
                        last = ts(OneA[:, slot, j, :], IOTA[:, :], PS[:, 1, c:c + 1], PS[:, 0, c:c + 1],
                                  ALU.is_equal, ALU.mult)
                    last.then_inc(hot_done, 1)

                def picks_of(pair):
                    nc.vector.tensor_copy(PS[:, :, :], PT[:, :, bass.ds(pair * 8, 8)])
                    dve.drain()

                def gate(four, slot, token):
                    dve.wait_ge(g_mm, four + 1)
                    rows = W[:, :, bass.ds(token, 4)]
                    tt(rows, rows, bank[2 + slot][:, :].rearrange("p (t i) -> p i t", t=4), ALU.mult).then_inc(g_used, 1)

                dve.wait_ge(mm_done, G(layer, AT_V, 0) * 8 + CREDIT)
                dve.wait_ge(evac_done, layer * (2 * P1_LAYER) + 2 * P1_LAYER + 2)
                n_pairs = T // 8
                picks_of(0)
                hot(0)

                def pair_body(pair, more):
                    base = layer * (2 * n_pairs)
                    hot(1)
                    gate(base + pair * 2, 0, pair * 8)
                    dve.drain()
                    if more:
                        picks_of(pair + 1)
                        hot(0)
                    gate(base + pair * 2 + 1, 1, pair * 8 + 4)

                with dve.Fori(0, n_pairs - 1) as pair:
                    pair_body(pair, True)
                pair_body(n_pairs - 1, False)
                dve.drain().then_inc(gated, 1)

                combine(layer, AT_V, P2_V, G_V, layer * 2 + 1)

            norm(2 * LAYERS, None, None)
            dve.wait_ge(final_in, 16)
            for a in range(TT):
                stt(H[:, a, :], H[:, a, :], STAT[:, 3, a:a + 1], FG[:, :], ALU.mult, ALU.mult).then_inc(out_ready, 1)

        @block.tensor
        def _(pe):
            mm = nc.tensor.matmul
            pe.sem_inc(mm_done, CREDIT)
            pe.wait_ge(const_in, 32)

            def p1_quarter(g, p1g, q):
                t, kq = q // 4, q % 4
                if kq == 0:
                    pe.wait_ge(evac_done, p1g * 2 + t + 1)
                pe.wait_ge(lo_done, g * 8 + q + 1 + CREDIT)
                for j in range(4):
                    k = kq * 4 + j
                    whi, wlo = HI[:, kq, j * P:(j + 1) * P], LO[:, kq, j * P:(j + 1) * P]
                    mm(bank[t][:, 0:T], whi, Xhi[:, k, :], start=k == 0, stop=False)
                    mm(bank[t][:, 0:T], whi, Xlo[:, k, :], start=False, stop=False)
                    last = mm(bank[t][:, 0:T], wlo, Xhi[:, k, :], start=False, stop=k == KT - 1)
                last.then_inc(mm_done, 1)

            def p1(layer, phase, p1_base, first, end):
                with pe.Fori(first, end) as i:
                    for q in range(8):
                        p1_quarter(G(layer, phase, i), layer * P1_LAYER + p1_base + i, q)

            def p2_group(layer, phase, p2_base, i, start, stop):
                g = G(layer, phase, i)
                for q in range(8):
                    t, c = q // 4, q % 4
                    if c == 0:
                        pe.wait_ge(ylo_done, layer * (2 * P2_LAYER) + (i * 2 + (2 * p2_base + t + 1)))
                    pe.wait_ge(lo_done, g * 8 + q + 1 + CREDIT)
                    for a in range(TT):
                        yhi, ylo = Yhi[:, t, a * P:(a + 1) * P], Ylo[:, t, a * P:(a + 1) * P]
                        dst = bank[a * 4 + c][:, :]
                        mm(dst, yhi, HI[:, c, :], start=start and t == 0, stop=False)
                        mm(dst, yhi, LO[:, c, :], start=False, stop=False)
                        last = mm(dst, ylo, HI[:, c, :], start=False, stop=stop and t == 1)
                    last.then_inc(mm_done, 1)

            def p2(layer, phase, p2_base, n_groups):
                p2_group(layer, phase, p2_base, 0, True, False)
                with pe.Fori(1, n_groups - 1) as i:
                    p2_group(layer, phase, p2_base, i, False, False)
                p2_group(layer, phase, p2_base, n_groups - 1, False, True)

            def transposes(number):
                for k in range(KT):
                    if k % 8 == 0:
                        pe.wait_ge(xn_dve, number * 2 + k // 8 + 1)
                        pe.wait_ge(xn_act, number * 2 + k // 8 + 1)
                    if k >= 8:
                        pe.wait_ge(xlo_done, number * KT + k - 8 + 1)
                    for a in range(TT):
                        last = nc.tensor.transpose(bank[k % 8][:, a * P:(a + 1) * P],
                                                   XN[:, a, k * P:(k + 1) * P], IDENT[:, :])
                    last.then_inc(tr_done, 1)
                stand(pe, xlo_done, number * KT + KT)

            with pe.Fori(0, LAYERS) as layer:
                transposes(layer * 2)
                p1(layer, AT_IN, P1_IN, 0, 6)
                pe.wait_ge(pool_rows, layer + 1)
                for n in range(POOL_TILES):
                    last = mm(pool_out(n), PAR[:, C_PW + n * P:C_PW + (n + 1) * P], W[:, LNY0 + n, :], start=True, stop=True)
                last.then_inc(pool_mm, 1)
                p1(layer, AT_IN, P1_IN, 6, G_IN)
                pe.wait_ge(conf_rows, layer * 6 + 6)
                for c in range(3):
                    mm(bank[2 + c][:, :], ONES[:, :], flat(C0 + 2 * c, 2), start=True, stop=True).then_inc(mean_mm, 1)
                for c in range(3):
                    pe.wait_ge(sq_done, layer * 3 + c + 1)
                    if c == 0:
                        pe.wait_ge(pool_used, layer + 1)
                    mm(bank[5 + c][:, :], ONES[:, :], flat(SQ0 + 2 * c, 2), start=True, stop=True).then_inc(var_mm, 1)
                p2(layer, AT_OUT, P2_OUT, G_OUT)
                transposes(layer * 2 + 1)

                pe.wait_ge(keys_in, layer * 16 + 16)

                def scores(i):
                    pe.wait_ge(evac_done, layer * (2 * P1_LAYER) + (i * 2 + (2 * P1_Q + 2)))
                    pe.wait_ge(s_out, layer * HEADS + i)
                    for a in range(TT):
                        for j in range(2):
                            keys_of = KEY[:, bass.ds(i * 2 + (j - 2), 1), :].rearrange("p a n -> p (a n)")
                            last = mm(bank[2][:, (a * 2 + j) * KEYS:(a * 2 + j + 1) * KEYS],
                                      W[:, QT0 + j, a * P:(a + 1) * P], keys_of, start=True, stop=True)
                    last.then_inc(s_mm, 1)

                def q_group(phase, p1_base, i, head):
                    for q in range(8):
                        p1_quarter(G(layer, phase, i), layer * P1_LAYER + p1_base + i, q)
                        if q == 3 and head is not None:
                            scores(head)

                q_group(AT_Q, P1_Q, 0, None)
                with pe.Fori(1, G_Q) as i:
                    q_group(AT_Q, P1_Q, i, i)
                q_group(AT_U, P1_U, 0, HEADS)
                p1(layer, AT_U, P1_U, 1, U_PICKS)
                pe.wait_ge(gates_done, layer + 1)
                for n in range(3):
                    for a in range(TT):
                        last = nc.tensor.transpose(bank[2 + n][:, a * P:(a + 1) * P], PK[:, n, a, :], IDENT[:, :])
                    last.then_inc(pt_mm, 1)
                p1(layer, AT_U, P1_U, U_PICKS, G_U)

                stand(pe, picks_done, layer + 1)
                with pe.Fori(0, T // 8) as pair:
                    for slot in range(2):
                        four = layer * (T // 4) + (pair * 2 + slot)
                        pe.wait_ge(hot_done, four + 1)
                        pe.wait_ge(g_used, four + (1 - 2 + 2))
                        for j in range(4):
                            last = mm(bank[2 + slot][:, j * P:(j + 1) * P], OneA[:, slot, j, :], OneB[:, slot, j, :],
                                      start=True, stop=True)
                        last.then_inc(g_mm, 1)
                p2(layer, AT_V, P2_V, G_V)


def _layout(inputs):
    f = {k: np.asarray(v) for k, v in inputs.items()}
    L = LAYERS

    def column_tiles(w):
        n = w.shape[2] // P
        return w.reshape(L, KT, P, n, P).transpose(0, 3, 2, 1, 4)

    win = column_tiles(f["w_in"])[:, WIN_ORDER]
    params = np.concatenate([
        f["norm1_g"].reshape(L, KT, P).transpose(0, 2, 1),
        f["norm2_g"].reshape(L, KT, P).transpose(0, 2, 1),
        f["pool_scale"].reshape(L, POOL_TILES, P).transpose(0, 2, 1),
        f["sconv_w"].reshape(L, SCONV_K * SCONV_TILES, P).transpose(0, 2, 1),
        f["conf_w"].reshape(L, CONF_K, CONF_TILES, P).transpose(0, 3, 2, 1).reshape(L, P, CONF_TILES * CONF_K),
        f["conf_b"].reshape(L, CONF_TILES, P).transpose(0, 2, 1),
        f["conf_ln_g"].reshape(L, CONF_TILES, P).transpose(0, 2, 1),
        f["conf_ln_b"].reshape(L, CONF_TILES, P).transpose(0, 2, 1),
        f["pool_w"].transpose(0, 2, 1, 3).reshape(L, P, POOL_TILES * P),
    ], axis=2)
    keys = np.stack([f["peer_k1"], f["peer_k2"]], axis=2)
    u = f["peer_u"].reshape(L, KEYS, KEYS, KT, P).transpose(0, 2, 4, 3, 1)
    v = f["peer_v"].reshape(L, KEYS, KEYS, D).transpose(0, 2, 1, 3)
    count = np.minimum(np.arange(1, T + 1)[None, :], np.array(WINDOWS)[:, None])
    c = np.ascontiguousarray
    return {
        "x": c(f["x"].reshape(T, D)),
        "win": c(win).reshape(L * 2 * G_IN, P, D),
        "wout": c(f["w_out"]).reshape(L * 2 * G_OUT, P, D),
        "wq": c(column_tiles(f["peer_wq"])).reshape(L * 2 * G_Q, P, D),
        "ut": c(u).reshape(L * W_TILES, P, D),
        "vt": c(v).reshape(L * W_TILES, P, D),
        "params": c(params),
        "keys": c(keys.transpose(0, 4, 1, 2, 3).reshape(L, P, 2 * HEADS * KEYS)),
        "final_g": c(f["final_g"]),
        "iota": np.broadcast_to(np.arange(P, dtype=np.float32), (P, P)).copy(),
        "ident": np.eye(P, dtype=np.float32),
        "invcnt": np.broadcast_to((1.0 / count).astype(np.float32).reshape(1, -1), (P, POOL_TILES * T)).copy(),
    }


def kernel(**inputs):
    import concourse.bacc as bacc
    from concourse.bass_utils import run_bass_kernel_spmd

    nc = bacc.Bacc("TRN2", target_bir_lowering=False, num_devices=1)
    arrays = _layout(inputs)
    args = [nc.dram_tensor(f"in_{n}", a.shape, F32, kind="ExternalInput").ap() for n, a in arrays.items()]
    out = nc.dram_tensor("out", (1, T, D), F32, kind="ExternalOutput").ap()
    build(nc, *args, out)
    result = run_bass_kernel_spmd(nc, [{f"in_{n}": a for n, a in arrays.items()}], core_ids=[0])
    return np.array(result.results[0]["out"])
```

```python
import numpy as np
import concourse.bass as bass
from concourse import mybir
from contextlib import ExitStack

F32 = mybir.dt.float32
F32R = mybir.dt.float32r
U32 = mybir.dt.uint32
ACT = mybir.ActivationFunctionType
ALU = mybir.AluOpType
AX = mybir.AxisListType

P = 128
T = 256
D = 2048
LAYERS = 2
TT = T // P
KT = D // P
POOL_TILES, SCONV_TILES, CONF_TILES = 4, 6, 6
SCONV_K, CONF_K = 3, 31
WINDOWS = (2, 4, 8, 16)
HEADS, TOPK, KEYS = 8, 16, 128
PICKS = HEADS * TOPK
EPS = 1e-6
NEG = -3.0e38

WIN_ORDER = (list(range(4)) + [n for i in range(6) for n in (22 + i, 28 + i)]
             + list(range(4, 10)) + list(range(16, 22)) + list(range(10, 16)))

G_IN, G_OUT, G_Q, G_U, G_V = 17, 8, 8, 64, 64
AT_IN = 0
AT_OUT = AT_IN + G_IN
AT_Q = AT_OUT + G_OUT
AT_U = AT_Q + G_Q
AT_V = AT_U + G_U
G_LAYER = AT_V + G_V
P1_IN, P1_Q, P1_U, P1_LAYER = 0, G_IN, G_IN + G_Q, G_IN + G_Q + G_U
P2_OUT, P2_V, P2_LAYER = 0, G_OUT, G_OUT + G_V

C_G1, C_G2 = 0, 16
C_PS = 32
C_SW = C_PS + POOL_TILES
C_CW = C_SW + SCONV_K * SCONV_TILES
C_CB = C_CW + CONF_TILES * CONF_K
C_LG = C_CB + CONF_TILES
C_LB = C_LG + CONF_TILES
N_PAR = C_LB + CONF_TILES

W_TILES = 128
Y0 = 0
XN0 = 16
Z0 = 32
ZC0 = Z0 + 4
ZH0, ZGC0, ZGB0 = Z0 + 16, Z0 + 22, Z0 + 28
PPAD0, XPAD0, SA0, SB0 = 66, 73, 78, 83
U0, ACC0, C0, XC0, SQ0, SACC0, INV0, LNY0, PW0 = 88, 90, 92, 98, 104, 110, 116, 120, 126
JUNK0 = 98
KEY0, QT0, S0 = 0, 8, 112
PP, XP, UP = SCONV_K - 1 + T + 2, 16 + T, 32 + T

TOPK_Q = 3
TOPK_U = TT * HEADS - TOPK_Q
U_TOPK0 = 1
U_EXP = 28
U_PICKS = 31
U_G0 = 32
DIRECT = 2 * U_EXP
assert U_TOPK0 + 2 * TOPK_U < U_EXP and (G_U - U_G0) * 8 == T
CREDIT = 8


def build(nc, x, win, wout, wq, ut, vt, params, keys, final_g, iota, ident, invcnt, poolw, out):
    hs = nc.dram_tensor("h_saved_rows", (P, TT, D), F32, kind="Internal").ap()
    ctx = ExitStack()
    with ctx:
        cursor = [(nc.sbuf_base + 63) // 64 * 64]

        def region(nbytes):
            at = cursor[0]
            cursor[0] += (nbytes + 31) // 32 * 32
            return at

        def sb(name, shape, dt, at=None):
            nbytes = 4 * int(np.prod(shape[1:]))
            return nc.alloc_sbuf_tensor_at(name, shape, dt, offset=region(nbytes) if at is None else at)

        def sem(name):
            return ctx.enter_context(nc.semaphore(name))

        W = sb("W", [P, W_TILES, T], F32)
        at_xa, at_xb = region(16384), region(16384)
        Xhi = sb("Xhi", [P, KT, T], F32R, at_xa)
        Xlo = sb("Xlo", [P, KT, T], F32R, at_xb)
        H = sb("H", [P, TT, D], F32, at_xa)
        Yhi = sb("Yhi", [P, 2, T], F32R, at_xb)
        Ylo = sb("Ylo", [P, 2, T], F32R, at_xb + 2048)
        FG = sb("FG", [P, D], F32, at_xb)
        RAW = sb("RAW", [P, 4, 1024], F32)
        HI = sb("HI", [P, 4, 512], F32R)
        LO = sb("LO", [P, 4, 512], F32R)
        PAR = sb("PAR", [P, N_PAR], F32)
        IOTA = sb("IOTA", [P, P], F32)
        IDENT = sb("IDENT", [P, P], F32)
        ONES = sb("ONES", [P, P], F32)
        at_top = region(4096)
        CAND = sb("CAND", [P, 256], F32, at_top)
        CAND2 = sb("CAND2", [P, 256], F32, at_top + 1024)
        EQ1 = sb("EQ1", [P, TOPK, TOPK], F32, at_top + 2048)
        EQ2 = sb("EQ2", [P, TOPK, TOPK], F32, at_top + 3072)
        PT = sb("PT", [P, 3, T], F32, at_top)
        at_sc = region(2048)
        SC = sb("SC", [P, 2, KEYS], F32, at_sc)
        SC2 = sb("SC2", [P, 2, KEYS], F32, at_sc + 1024)
        GT = sb("GT", [P, 2, T], F32, at_sc)
        TV = sb("TV", [P, 2, TOPK], F32)
        TI = sb("TI", [P, 2, TOPK], U32)
        TIF = sb("TIF", [P, 2, TOPK], F32)
        BV = sb("BV", [P, TOPK], F32)
        BI = sb("BI", [P, TOPK], U32)
        BAB = sb("BAB", [P, 2, TOPK], U32)
        at_pk = region(4096)
        PK = sb("PK", [P, 3, TT, PICKS], F32, at_pk)
        OneA = sb("OneA", [P, 4, P], F32, at_pk)
        OneB = sb("OneB", [P, 4, P], F32, at_pk + 2048)
        SUMS = sb("SUMS", [P, TT * HEADS], F32)
        STAT = sb("STAT", [P, 8, TT], F32)
        WC = sb("WC", [P, CONF_K + 1], F32)
        PS = sb("PS", [P, 3, 8], F32)
        assert cursor[0] <= nc.sbuf_usable_end, (cursor[0], nc.sbuf_usable_end)
        bank = [ctx.enter_context(nc.psum_tensor(f"bank{i}", [P, 512], F32)) for i in range(8)]

        def tiles(first, n):
            return W[:, first:first + n, :]

        def flat(first, n):
            return W[:, first:first + n, :].rearrange("p a t -> p (a t)")

        XN = flat(XN0, 16).rearrange("p (a d) -> p a d", a=TT)
        PPAD = flat(PPAD0, 7)[:, 0:SCONV_TILES * PP].rearrange("p (a t) -> p a t", t=PP)
        XPAD = flat(XPAD0, 5)[:, 0:POOL_TILES * XP].rearrange("p (a t) -> p a t", t=XP)
        SA = flat(SA0, 5)[:, 0:POOL_TILES * XP].rearrange("p (a t) -> p a t", t=XP)
        SB = flat(SB0, 5)[:, 0:POOL_TILES * XP].rearrange("p (a t) -> p a t", t=XP)
        UPAD = flat(U0, 2)[:, 0:UP]
        KEY = flat(KEY0, 8).rearrange("p (j n) -> p j n", n=KEYS)
        SBUFQ = flat(S0, 16).rearrange("p (a j n) -> p a j n", a=TT, n=KEYS)

        def pool_out(n):
            return bank[6 + n // 2][:, (n % 2) * T:(n % 2 + 1) * T]

        const_in = sem("const_in")
        x_in = sem("x_in")
        final_in = sem("final_in")
        par_in = sem("par_in")
        inv_in = sem("inv_in")
        keys_in = sem("keys_in")
        raw_in = [sem(f"raw_in{s}") for s in range(4)]
        hi_done = sem("hi_done")
        lo_done = sem("lo_done")
        mm_done = sem("mm_done")
        evac_done = sem("evac_done")
        yhi_done = sem("yhi_done")
        ylo_done = sem("ylo_done")
        h_ready = sem("h_ready")
        h_saved = sem("h_saved")
        h_back = sem("h_back")
        ssq_done = sem("ssq_done")
        var_done = sem("var_done")
        std_done = sem("std_done")
        rstd_done = sem("rstd_done")
        xn_act = sem("xn_act")
        xn_dve = sem("xn_dve")
        tr_done = sem("tr_done")
        xhi_done = sem("xhi_done")
        xlo_done = sem("xlo_done")
        pool_rows = sem("pool_rows")
        pool_mm = sem("pool_mm")
        pool_used = sem("pool_used")
        conf_rows = sem("conf_rows")
        mean_mm = sem("mean_mm")
        cent_done = sem("cent_done")
        sq_done = sem("sq_done")
        var_mm = sem("var_mm")
        lstd_done = sem("lstd_done")
        lny_done = sem("lny_done")
        sig_done = sem("sig_done")
        mixed = sem("mixed")
        s_mm = sem("s_mm")
        s_out = sem("s_out")
        topk_done = sem("topk_done")
        exp_done = sem("exp_done")
        gates_done = sem("gates_done")
        pt_mm = sem("pt_mm")
        hot_done = sem("hot_done")
        g_mm = sem("g_mm")
        g_used = sem("g_used")
        gated = sem("gated")
        ones_in = sem("ones_in")
        gm_done = sem("gm_done")
        passed = sem("passed")
        out_ready = sem("out_ready")
        out_done = sem("out_done")

        block = ctx.enter_context(nc.Block())

        def stand(eng, semaphore, value):
            eng.wait_ge(semaphore, value)
            eng.sem_inc(passed, 1)

        def G(layer, phase, i):
            return layer * G_LAYER + phase + i

        @block.sync
        def _(sp):
            def load(layer, src, per_layer, phase, n_groups):
                with sp.Fori(0, n_groups) as i:
                    for s in range(4):
                        sp.wait_ge(lo_done, G(layer, phase, i) * 8 + 2 * s + 2)
                        sp.dma_start(
                            RAW[:, s, :],
                            src[bass.ds(layer * per_layer + i * 2 + s // 2, 1), :,
                                (s % 2) * 1024:(s % 2 + 1) * 1024].rearrange("a p n -> p (a n)"),
                        ).then_inc(raw_in[s], 16)

            with sp.Fori(0, LAYERS) as layer:
                load(layer, win, 2 * G_IN, AT_IN, G_IN)
                load(layer, wout, 2 * G_OUT, AT_OUT, G_OUT)
                load(layer, wq, 2 * G_Q, AT_Q, G_Q)
                load(layer, ut, 2 * G_U, AT_U, G_U)
                load(layer, vt, 2 * G_V, AT_V, G_V)
            for a in range(TT):
                sp.wait_ge(out_ready, a + 1)
                sp.dma_start(out[0, a * P:(a + 1) * P, :], H[:, a, :]).then_inc(out_done, 16)
            sp.wait_ge(out_done, 16 * TT)

        @block.gpsimd
        def _(pool):
            pool.dma_start(IOTA[:, :], iota).then_inc(const_in, 16)
            pool.dma_start(IDENT[:, :], ident).then_inc(const_in, 16)

            def save(norm):
                stand(pool, h_ready, norm + 1)
                pool.dma_start(hs, H[:, :, :]).then_inc(h_saved, 16)

            def bring_back(norm, first_group):
                stand(pool, mm_done, first_group * 8 + CREDIT)
                stand(pool, h_saved, norm * 16 + 16)
                pool.dma_start(H[:, :, :], hs).then_inc(h_back, 16)

            with pool.Fori(0, LAYERS) as layer:
                stand(pool, h_ready, layer * 2 + 1)
                pool.dma_start(PAR[:, :], params[bass.ds(layer, 1), :, :].rearrange("a p n -> p (a n)")).then_inc(par_in, 16)
                save(layer * 2)
                pool.dma_start(flat(INV0, 4), invcnt).then_inc(inv_in, 16)
                pool.dma_start(flat(PW0, 2), poolw[bass.ds(layer, 1), :, :].rearrange("a p n -> p (a n)")).then_inc(inv_in, 16)
                bring_back(layer * 2, G(layer, AT_OUT, 0))
                save(layer * 2 + 1)
                pool.dma_start(flat(KEY0, 8), keys[bass.ds(layer, 1), :, :].rearrange("a p n -> p (a n)")).then_inc(keys_in, 16)
                stand(pool, rstd_done, layer * 2 + 2)
                nc.gpsimd.memset(flat(DIRECT, S0 - DIRECT), 1.0).then_inc(ones_in, 1)
                stand(pool, topk_done, layer + 1)
                nc.gpsimd.memset(flat(S0, W_TILES - S0), 1.0).then_inc(ones_in, 1)
                bring_back(layer * 2 + 1, G(layer, AT_V, 0))
            stand(pool, h_ready, 2 * LAYERS + 1)
            pool.dma_start(FG[:, :], final_g.unsqueeze(0).to_broadcast([P, D])).then_inc(final_in, 16)

        @block.scalar
        def _(act):
            act.dma_start(H[:, :, :], x.rearrange("(a p) d -> p a d", p=P)).then_inc(x_in, 16)

            def hi(g, q):
                if q % 2 == 0:
                    act.wait_ge(raw_in[q // 2], g * 16 + 16)
                act.wait_ge(mm_done, g * 8 + q + 5)
                nc.scalar.activation(HI[:, q % 4, :], RAW[:, q // 2, (q % 2) * 512:(q % 2 + 1) * 512],
                                     ACT.Copy).then_inc(hi_done, 1)

            def evac(g, t, dst, func):
                act.wait_ge(mm_done, g * 8 + 4 * t + 4 + CREDIT)
                nc.scalar.activation(dst, bank[t][:, 0:T], func).then_inc(evac_done, 1)

            def p1_group(g, before, after, first=0):
                for q in range(first, 4):
                    hi(g, q)
                if before:
                    before()
                for q in range(4, 8):
                    hi(g, q)
                after()

            def wtile(n):
                return W[:, bass.ds(n, 1), :].rearrange("p a t -> p (a t)")

            def norm(number, gain, par_value, g_next):
                if g_next is not None:
                    for q in range(4):
                        hi(g_next, q)
                act.wait_ge(h_ready, number + 1)
                nc.scalar.activation(flat(JUNK0, 8), H[:, 0, :], ACT.Square,
                                     accum_out=STAT[:, 0, 0:1]).then_inc(ssq_done, 1)
                act.wait_ge(var_done, number + 1)
                nc.scalar.activation(STAT[:, 2, :], STAT[:, 1, :], ACT.Sqrt).then_inc(std_done, 1)
                if gain is None:
                    return
                act.wait_ge(rstd_done, number + 1)
                for c in range(2):
                    nc.scalar.activation(XN[:, 1, c * 1024:(c + 1) * 1024], H[:, 1, c * 1024:(c + 1) * 1024],
                                         ACT.Copy, scale=STAT[:, 3, 1:2]).then_inc(xn_act, 1)
                act.wait_ge(h_saved, number * 16 + 16)
                act.wait_ge(xn_dve, number * 2 + 2)
                act.wait_ge(xn_act, number * 2 + 2)
                act.wait_ge(par_in, par_value)
                for k in range(KT):
                    act.wait_ge(tr_done, number * KT + k + 1)
                    nc.scalar.activation(Xhi[:, k, :], bank[2 + k % 6][:, 0:T],
                                         ACT.Copy, scale=PAR[:, gain + k:gain + k + 1]).then_inc(xhi_done, 1)

            def combine(layer, phase, n_groups, ready, ready_value, between):
                g = G(layer, phase, 0)
                for q in range(4):
                    hi(g, q)
                between()
                act.wait_ge(ready, ready_value)
                nc.scalar.activation(Yhi[:, 0, :], W[:, 0, :], ACT.Copy).then_inc(yhi_done, 1)
                act.wait_ge(mm_done, g * 8 + CREDIT)
                nc.scalar.activation(Yhi[:, 1, :], W[:, 1, :], ACT.Copy).then_inc(yhi_done, 1)
                for q in range(4, 8):
                    hi(g, q)
                with act.Fori(1, n_groups) as i:
                    g = G(layer, phase, i)
                    for t in range(2):
                        act.wait_ge(mm_done, g * 8 + 4 * t + 4)
                        nc.scalar.activation(Yhi[:, t, :], wtile(i * 2 + t), ACT.Copy).then_inc(yhi_done, 1)
                        for q in range(4 * t, 4 * t + 4):
                            hi(g, q)

            with act.Fori(0, LAYERS) as layer:
                norm(layer * 2, C_G1, layer * 16 + 16, G(layer, AT_IN, 0))

                act.preload_act_table(ACT.Sigmoid)

                def z(i, t):
                    return wtile(i * 2 + (Z0 + t))

                def in_group(i, prev_func, first=0):
                    g = G(layer, AT_IN, i)
                    before = None
                    if prev_func is not None:
                        def before():
                            evac(g - 1, 1, z(i, -1), prev_func)
                    p1_group(g, before, lambda: evac(g, 0, z(i, 0), ACT.Copy), first)

                in_group(0, None, 4)
                with act.Fori(1, 3) as i:
                    in_group(i, ACT.Copy)
                with act.Fori(3, 9) as i:
                    in_group(i, ACT.Sigmoid)
                with act.Fori(9, G_IN) as i:
                    in_group(i, ACT.Copy)
                evac(G(layer, AT_IN, G_IN - 1), 1, W[:, Z0 + 2 * G_IN - 1, :], ACT.Copy)

                def conformer_norm():
                    for c in range(3):
                        act.wait_ge(cent_done, layer * 3 + c + 1)
                        nc.scalar.activation(flat(SQ0 + 2 * c, 2), flat(XC0 + 2 * c, 2), ACT.Square).then_inc(sq_done, 1)
                    act.preload_act_table(ACT.Sqrt)
                    for c in range(3):
                        act.wait_ge(var_mm, layer * 3 + c + 1)
                        nc.scalar.activation(flat(SQ0 + 2 * c, 2), bank[5 + c][:, :], ACT.Sqrt, bias=EPS).then_inc(lstd_done, 1)
                    act.preload_act_table(ACT.Sigmoid)
                    for c in range(3):
                        act.wait_ge(lny_done, layer * 3 + c + 1)
                        nc.scalar.activation(flat(XC0 + 2 * c, 2), flat(LNY0 + 2 * c, 2), ACT.Sigmoid).then_inc(sig_done, 1)

                combine(layer, AT_OUT, G_OUT, mixed, layer + 1, conformer_norm)
                norm(layer * 2 + 1, C_G2, layer * 16 + 16, G(layer, AT_Q, 0))

                act.preload_act_table(ACT.Gelu)

                def evac_q(i, t):
                    if t == 0:
                        act.wait_ge(s_mm, layer * HEADS + i)
                    evac(G(layer, AT_Q, i), t, W[:, QT0 + t, :], ACT.Copy)

                p1_group(G(layer, AT_Q, 0), None, lambda: evac(G(layer, AT_Q, 0), 0, W[:, QT0, :], ACT.Copy), 4)
                with act.Fori(1, G_Q) as i:
                    p1_group(G(layer, AT_Q, i), lambda: evac_q(i - 1, 1), lambda: evac_q(i, 0))

                def u_evac(i, t, direct):
                    g = G(layer, AT_U, i)
                    if direct:
                        evac(g, t, wtile(i * 2 + t), ACT.Gelu)
                    else:
                        act.wait_ge(gm_done, layer * (W_TILES - DIRECT) + (i * 2 + (t + 1 - DIRECT)))
                        evac(g, t, GT[:, t, :], ACT.Gelu)

                def u_group(i, prev_direct, direct):
                    p1_group(G(layer, AT_U, i), lambda: u_evac(i - 1, 1, prev_direct), lambda: u_evac(i, 0, direct))

                p1_group(G(layer, AT_U, 0), lambda: evac_q(G_Q - 1, 1), lambda: u_evac(0, 0, True))
                with act.Fori(1, U_EXP) as i:
                    u_group(i, True, True)
                act.wait_ge(topk_done, layer + 1)
                gate_logits = PK[:, 0, :, :].rearrange("p a k -> p (a k)")
                nc.scalar.activation(gate_logits, gate_logits, ACT.Exp).then_inc(exp_done, 1)
                act.preload_act_table(ACT.Gelu)
                u_group(U_EXP, True, False)
                with act.Fori(U_EXP + 1, G_U) as i:
                    u_group(i, False, False)
                combine(layer, AT_V, G_V, gated, layer + 1, lambda: u_evac(G_U - 1, 1, False))

            norm(2 * LAYERS, None, None, None)

        @block.vector
        def _(dve):
            tt = nc.vector.tensor_tensor
            ts = nc.vector.tensor_scalar
            stt = nc.vector.scalar_tensor_tensor

            def lo(g, q):
                dve.wait_ge(hi_done, g * 8 + q + 1)
                tt(LO[:, q % 4, :], RAW[:, q // 2, (q % 2) * 512:(q % 2 + 1) * 512],
                   HI[:, q % 4, :].bitcast(F32), ALU.subtract).then_inc(lo_done, 1)

            def lo_group(g, side=None, first=0):
                for q in range(first, 8):
                    lo(g, q)
                    if side:
                        side(q)

            def plain(layer, phase, first, end):
                with dve.Fori(first, end) as i:
                    lo_group(G(layer, phase, i))

            def norm(number, gain, par_value, g_next):
                dve.wait_ge(h_ready, number + 1)
                nc.vector.tensor_tensor_reduce(out=XN[:, 0, :], in0=H[:, 1, :], in1=H[:, 1, :], scale=1.0,
                                               scalar=0.0, op0=ALU.mult, op1=ALU.add, accum_out=STAT[:, 0, 1:2])
                dve.drain()
                dve.wait_ge(ssq_done, number + 1)
                ts(STAT[:, 1, :], STAT[:, 0, :], 1.0 / D, EPS, ALU.mult, ALU.add).then_inc(var_done, 1)
                if g_next is not None:
                    for q in range(4):
                        lo(g_next, q)
                dve.wait_ge(std_done, number + 1)
                nc.vector.reciprocal(STAT[:, 3, :], STAT[:, 2, :])
                dve.drain()
                tt(STAT[:, 4, :], STAT[:, 3, :], STAT[:, 3, :], ALU.mult)
                dve.drain()
                tt(STAT[:, 5, :], STAT[:, 4, :], STAT[:, 1, :], ALU.mult)
                dve.drain()
                ts(STAT[:, 6, :], STAT[:, 5, :], -0.5, 1.5, ALU.mult, ALU.add)
                dve.drain()
                tt(STAT[:, 3, :], STAT[:, 3, :], STAT[:, 6, :], ALU.mult).then_inc(rstd_done, 1)
                dve.drain()
                if gain is None:
                    return
                for c in range(2):
                    ts(XN[:, 0, c * 1024:(c + 1) * 1024], H[:, 0, c * 1024:(c + 1) * 1024],
                       STAT[:, 3, 0:1], None, ALU.mult).then_inc(xn_dve, 1)
                dve.wait_ge(par_in, par_value)
                for k in range(KT):
                    dve.wait_ge(xhi_done, number * KT + k + 1)
                    stt(Xlo[:, k, :], bank[2 + k % 6][:, 0:T],
                        PAR[:, gain + k:gain + k + 1], Xhi[:, k, :].bitcast(F32),
                        ALU.mult, ALU.subtract).then_inc(xlo_done, 1)

            def y_lo(layer, number, tile, t):
                dve.wait_ge(yhi_done, layer * (2 * P2_LAYER) + number)
                tt(Ylo[:, t, :], W[:, bass.ds(tile, 1), :].rearrange("p a t -> p (a t)"),
                   Yhi[:, t, :].bitcast(F32), ALU.subtract).then_inc(ylo_done, 1)

            def combine(layer, phase, p2_base, n_groups, back, between):
                g = G(layer, phase, 0)
                for q in range(4):
                    lo(g, q)
                between()
                for t in range(2):
                    y_lo(layer, 2 * p2_base + t + 1, t, t)
                for q in range(4, 8):
                    lo(g, q)
                with dve.Fori(1, n_groups) as i:
                    for t in range(2):
                        y_lo(layer, i * 2 + (2 * p2_base + t + 1), i * 2 + t, t)
                        for q in range(4 * t, 4 * t + 4):
                            lo(G(layer, phase, i), q)
                dve.wait_ge(h_back, back * 16 + 16)
                for c in range(4):
                    dve.wait_ge(mm_done, G(layer, phase, n_groups) * 8 + c - 3 + CREDIT)
                    for a in range(TT):
                        rows = H[:, a, c * 512:(c + 1) * 512]
                        tt(rows, bank[a * 4 + c][:, :], rows, ALU.add)
                dve.drain().then_inc(h_ready, 1)

            dve.sem_inc(lo_done, CREDIT)
            dve.sem_inc(evac_done, 2)
            dve.sem_inc(gm_done, 2)
            dve.sem_inc(s_out, 1)
            nc.vector.memset(ONES[:, :], 1.0 / P)
            dve.wait_ge(x_in, 16)
            dve.sem_inc(h_ready, 1)
            dve.wait_ge(const_in, 32)

            with dve.Fori(0, LAYERS) as layer:
                norm(layer * 2, C_G1, layer * 16 + 16, G(layer, AT_IN, 0))

                def z_done(n):
                    return layer * (2 * P1_LAYER) + n + 1 + 2

                nc.vector.memset(PPAD[:, :, 0:SCONV_K - 1], 0.0)
                nc.vector.memset(XPAD[:, :, 0:16], 0.0)
                nc.vector.memset(SA[:, :, 0:16], 0.0)
                nc.vector.memset(SB[:, :, 0:16], 0.0)
                nc.vector.memset(UPAD[:, 0:32], 0.0)
                lo_group(G(layer, AT_IN, 0), None, 4)
                plain(layer, AT_IN, 1, 3)

                dve.wait_ge(evac_done, z_done(3))
                dve.wait_ge(inv_in, layer * 32 + 32)
                nc.vector.tensor_copy(XPAD[:, :, 16:XP], tiles(Z0, 4))
                dve.drain()
                steps = [(XPAD, SA, 0, 1), (SA, SB, 1, 2), (SB, SA, 2, 4), (SA, SB, 3, 8)]
                for src, dst, first, shift in steps:
                    tt(dst[:, first:4, 16:XP], src[:, first:4, 16:XP], src[:, first:4, 16 - shift:XP - shift], ALU.add)
                    dve.drain()
                    tt(tiles(SACC0 + first, 1).rearrange("p a t -> p (a t)"), dst[:, first, 16:XP],
                       W[:, INV0 + first, :], ALU.mult)
                    dve.drain()
                tt(tiles(LNY0, 4), tiles(SACC0, 4), tiles(Z0, 4), ALU.subtract).then_inc(pool_rows, 1)

                lo_group(G(layer, AT_IN, 3))

                with dve.Fori(0, CONF_TILES) as j:
                    accs = [W[:, ACC0, :], W[:, ACC0 + 1, :]]

                    def taps(pair):
                        for k in (2 * pair, 2 * pair + 1):
                            if k >= CONF_K:
                                continue
                            src, acc = UPAD[:, 2 + k:2 + k + T], accs[k % 2]
                            if k == 0:
                                ts(acc, src, WC[:, 0:1], WC[:, CONF_K:CONF_K + 1], ALU.mult, ALU.add)
                            elif k == 1:
                                ts(acc, src, WC[:, 1:2], None, ALU.mult)
                            else:
                                stt(acc, src, WC[:, k:k + 1], acc, ALU.mult, ALU.add)
                        dve.drain()

                    def first_side(q):
                        if q == 0:
                            dve.wait_ge(evac_done, layer * (2 * P1_LAYER) + j * 2 + (4 + 2 + 2))
                            pair = W[:, bass.ds(j * 2 + ZC0, 2), :]
                            tt(UPAD[:, 32:UP], pair[:, 0, :], pair[:, 1, :], ALU.mult)
                            nc.vector.tensor_copy(WC[:, 0:CONF_K], PAR[:, bass.ds(j * CONF_K + C_CW, CONF_K)])
                            nc.vector.tensor_copy(WC[:, CONF_K:CONF_K + 1], PAR[:, bass.ds(j + C_CB, 1)])
                            dve.drain()
                        taps(q)

                    def second_side(q):
                        taps(8 + q)
                        if q == 7:
                            tt(W[:, bass.ds(j + C0, 1), :].rearrange("p a t -> p (a t)"), accs[0], accs[1],
                               ALU.add).then_inc(conf_rows, 1)
                            dve.drain()

                    lo_group(G(layer, AT_IN, j * 2 + 4), first_side)
                    lo_group(G(layer, AT_IN, j * 2 + 5), second_side)
                lo_group(G(layer, AT_IN, G_IN - 1))

                dve.wait_ge(pool_mm, layer + 1)
                for n in range(POOL_TILES):
                    last = ts(W[:, Y0 + n, :], pool_out(n), PAR[:, C_PS + n:C_PS + n + 1], None, ALU.mult)
                last.then_inc(pool_used, 1)

                def mixer_rest():
                    for c in range(3):
                        dve.wait_ge(mean_mm, layer * 3 + c + 1)
                        tt(flat(XC0 + 2 * c, 2), flat(C0 + 2 * c, 2), bank[2 + c][:, :], ALU.subtract).then_inc(cent_done, 1)
                    dve.wait_ge(evac_done, z_done(2 * G_IN - 1))
                    tt(PPAD[:, :, 2:2 + T], tiles(ZGC0, 6), tiles(ZH0, 6), ALU.mult)
                    dve.drain()
                    for k in range(SCONV_K):
                        for n in range(SCONV_TILES):
                            w = PAR[:, C_SW + k * SCONV_TILES + n:C_SW + k * SCONV_TILES + n + 1]
                            acc, src = W[:, SACC0 + n, :], PPAD[:, n, k:k + T]
                            if k == 0:
                                ts(acc, src, w, None, ALU.mult)
                            else:
                                stt(acc, src, w, acc, ALU.mult, ALU.add)
                        dve.drain()
                    tt(tiles(Y0 + POOL_TILES, 6), tiles(SACC0, 6), tiles(ZGB0, 6), ALU.mult)
                    for c in range(3):
                        dve.wait_ge(lstd_done, layer * 3 + c + 1)
                        nc.vector.reciprocal(flat(C0 + 2 * c, 2), flat(SQ0 + 2 * c, 2))
                        dve.drain()
                        tt(flat(XC0 + 2 * c, 2), flat(XC0 + 2 * c, 2), flat(C0 + 2 * c, 2), ALU.mult)
                        dve.drain()
                        for n in (2 * c, 2 * c + 1):
                            last = ts(W[:, LNY0 + n, :], W[:, XC0 + n, :], PAR[:, C_LG + n:C_LG + n + 1],
                                      PAR[:, C_LB + n:C_LB + n + 1], ALU.mult, ALU.add)
                        dve.drain().then_inc(lny_done, 1)
                    for c in range(3):
                        dve.wait_ge(sig_done, layer * 3 + c + 1)
                        tt(flat(Y0 + 10 + 2 * c, 2), flat(LNY0 + 2 * c, 2), flat(XC0 + 2 * c, 2), ALU.mult)
                    dve.drain().then_inc(mixed, 1)

                combine(layer, AT_OUT, P2_OUT, G_OUT, layer * 2, mixer_rest)
                norm(layer * 2 + 1, C_G2, layer * 16 + 16, G(layer, AT_Q, 0))

                def scores_out(head, count):
                    dve.wait_ge(s_mm, count)
                    nc.vector.tensor_copy(SBUFQ[:, :, bass.ds(head * 2, 2), :],
                                          bank[2][:, :].rearrange("p (a j n) -> p a j n", a=TT, n=KEYS)
                                          ).then_inc(s_out, 1)

                def topk(b, group_a, group_b, end_a, end_b):
                    def half_topk(h):
                        first, second = slice(0, 8), slice(8, 16)
                        nc.vector.max(TV[:, h, first], SC[:, h, :])
                        dve.drain()
                        nc.vector.max_index(TI[:, h, first], TV[:, h, first], SC[:, h, :])
                        nc.vector.match_replace(SC2[:, h, :], TV[:, h, first], SC[:, h, :], NEG)
                        dve.drain()
                        nc.vector.max(TV[:, h, second], SC2[:, h, :])
                        dve.drain()
                        nc.vector.max_index(TI[:, h, second], TV[:, h, second], SC2[:, h, :])

                    def side_a(q):
                        if q == 0:
                            dve.drain()
                            nc.vector.tensor_copy(
                                SC[:, :, :],
                                flat(S0, 16)[:, bass.ds(b * (2 * KEYS), 2 * KEYS)].rearrange("p (j n) -> p j n", n=KEYS))
                            dve.drain()
                        elif q == 2:
                            half_topk(0)
                        elif q == 4:
                            half_topk(1)
                        elif q == 6:
                            dve.drain()
                            nc.vector.tensor_copy(TIF[:, :, :], TI[:, :, :])
                            tt(CAND[:, :].rearrange("p (a b) -> p a b", b=TOPK),
                               TV[:, 0, :].unsqueeze(2).to_broadcast([P, TOPK, TOPK]),
                               TV[:, 1, :].unsqueeze(1).to_broadcast([P, TOPK, TOPK]), ALU.add)
                            dve.drain()

                    def chosen(h, eq):
                        tt(eq[:, :, :], BAB[:, h, :].unsqueeze(2).to_broadcast([P, TOPK, TOPK]),
                           IOTA[:, 0:TOPK].unsqueeze(1).to_broadcast([P, TOPK, TOPK]), ALU.is_equal)

                    def times_keys(h, eq):
                        tt(eq[:, :, :], eq[:, :, :], TIF[:, h, :].unsqueeze(1).to_broadcast([P, TOPK, TOPK]), ALU.mult)

                    def summed(h, eq):
                        nc.vector.tensor_reduce(
                            PK[:, 1 + h, :, :].rearrange("p a k -> p (a k)")[:, bass.ds(b * TOPK, TOPK)],
                            eq[:, :, :], AX.X, ALU.add)

                    def side_b(q):
                        if q == 0:
                            nc.vector.max(BV[:, 0:8], CAND[:, :])
                            dve.drain()
                            nc.vector.max_index(BI[:, 0:8], BV[:, 0:8], CAND[:, :])
                            nc.vector.match_replace(CAND2[:, :], BV[:, 0:8], CAND[:, :], NEG)
                            dve.drain()
                        elif q == 1:
                            nc.vector.max(BV[:, 8:16], CAND2[:, :])
                            dve.drain()
                            nc.vector.max_index(BI[:, 8:16], BV[:, 8:16], CAND2[:, :])
                            dve.drain()
                        elif q == 2:
                            ts(BAB[:, 0, :], BI[:, :], 4, None, ALU.logical_shift_right)
                            ts(BAB[:, 1, :], BI[:, :], 15, None, ALU.bitwise_and)
                            ts(PK[:, 0, :, :].rearrange("p a k -> p (a k)")[:, bass.ds(b * TOPK, TOPK)],
                               BV[:, :], BV[:, 0:1], None, ALU.subtract)
                            dve.drain()
                        elif q == 3:
                            chosen(0, EQ1)
                            chosen(1, EQ2)
                            dve.drain()
                        elif q == 5:
                            times_keys(0, EQ1)
                            times_keys(1, EQ2)
                            dve.drain()
                        elif q == 6:
                            summed(0, EQ1)
                            summed(1, EQ2)
                            dve.drain()

                    lo_group(group_a, side_a)
                    end_a()
                    lo_group(group_b, side_b)
                    end_b()

                def nothing():
                    pass

                lo_group(G(layer, AT_Q, 0), None, 4)
                lo_group(G(layer, AT_Q, 1))
                scores_out(0, layer * HEADS + 1)
                with dve.Fori(0, TOPK_Q) as b:
                    topk(b, G(layer, AT_Q, b * 2 + 2), G(layer, AT_Q, b * 2 + 3),
                         lambda: scores_out(b * 2 + 1, layer * HEADS + (b * 2 + 2)),
                         lambda: scores_out(b * 2 + 2, layer * HEADS + (b * 2 + 3)))
                lo_group(G(layer, AT_U, 0))
                scores_out(HEADS - 1, layer * HEADS + HEADS)
                dve.drain()
                with dve.Fori(0, TOPK_U) as b:
                    topk(b + TOPK_Q, G(layer, AT_U, b * 2 + U_TOPK0), G(layer, AT_U, b * 2 + U_TOPK0 + 1),
                         nothing, nothing)
                dve.drain().then_inc(topk_done, 1)
                plain(layer, AT_U, U_TOPK0 + 2 * TOPK_U, U_EXP + 1)

                dve.wait_ge(exp_done, layer + 1)
                by_head = PK[:, 0, :, :].rearrange("p a (h k) -> p (a h) k", k=TOPK)
                nc.vector.tensor_reduce(SUMS[:, :], by_head, AX.X, ALU.add)
                dve.drain()
                nc.vector.reciprocal(SUMS[:, :], SUMS[:, :])
                dve.drain()
                tt(by_head, by_head, SUMS[:, :].unsqueeze(2).to_broadcast([P, TT * HEADS, TOPK]), ALU.mult).then_inc(gates_done, 1)

                def activation_in(i, t):
                    dve.wait_ge(evac_done, layer * (2 * P1_LAYER) + (i * 2 + (2 * P1_U + t + 3)))
                    rows = W[:, bass.ds(i * 2 + t, 1), :].rearrange("p a t -> p (a t)")
                    tt(rows, rows, GT[:, t, :], ALU.mult).then_inc(gm_done, 1)

                def activations_in(i):
                    def side(q):
                        if q in (2, 6):
                            activation_in(i - 1, q // 4)
                    return side

                def hot(slot):
                    tt(OneB[:, :, :], IOTA[:, :].unsqueeze(1).to_broadcast([P, 4, P]),
                       PS[:, 2, slot * 4:slot * 4 + 4].unsqueeze(2).to_broadcast([P, 4, P]), ALU.is_equal)
                    for c in range(slot * 4, slot * 4 + 4):
                        last = ts(OneA[:, c % 4, :], IOTA[:, :], PS[:, 1, c:c + 1], PS[:, 0, c:c + 1],
                                  ALU.is_equal, ALU.mult)
                    last.then_inc(hot_done, 1)

                def gate(token, four, slot, i):
                    dve.wait_ge(g_mm, four)
                    dve.wait_ge(gm_done, layer * (W_TILES - DIRECT) + i)
                    rows = W[:, :, bass.ds(token, 4)]
                    tt(rows, rows, bank[2 + slot][:, :].rearrange("p (t i) -> p i t", t=4), ALU.mult).then_inc(g_used, 1)

                def g_group(n, first):
                    i = n + U_G0
                    fours = layer * (T // 4) + n * 2

                    def side(q):
                        if q == 1:
                            if not first:
                                gate(n * 8 - 4, fours, 1, n * 2 + (2 * U_G0 - 2 - DIRECT + 2))
                            nc.vector.tensor_copy(PS[:, :, :], PT[:, :, bass.ds(n * 8, 8)])
                            dve.drain()
                            hot(0)
                        elif q == 2:
                            if not first:
                                dve.wait_ge(g_used, fours)
                            activation_in(i - 1, 0)
                        elif q == 5:
                            gate(n * 8, fours + 1, 0, n * 2 + (2 * U_G0 - 1 - DIRECT + 2))
                            hot(1)
                        elif q == 6:
                            dve.wait_ge(g_used, fours + 1)
                            activation_in(i - 1, 1)
                    lo_group(G(layer, AT_U, i), side)

                stand(dve, ones_in, layer * 2 + 2)
                with dve.Fori(U_EXP + 1, U_PICKS) as i:
                    lo_group(G(layer, AT_U, i), activations_in(i))

                def picks_in(q):
                    if q == 3:
                        for n in range(3):
                            dve.wait_ge(pt_mm, layer * 3 + n + 1)
                            nc.vector.tensor_copy(PT[:, n, :], bank[2 + n][:, 0:T])
                        dve.drain()
                    activations_in(U_PICKS)(q)
                lo_group(G(layer, AT_U, U_PICKS), picks_in)

                g_group(0, True)
                with dve.Fori(1, G_U - U_G0) as n:
                    g_group(n, False)
                gate(T - 4, layer * (T // 4) + T // 4, 1, 2 * (G_U - 1) - DIRECT + 2)
                dve.drain().then_inc(gated, 1)

                def last_activations():
                    activation_in(G_U - 1, 0)
                    activation_in(G_U - 1, 1)
                combine(layer, AT_V, P2_V, G_V, layer * 2 + 1, last_activations)

            norm(2 * LAYERS, None, None, None)
            dve.wait_ge(final_in, 16)
            for a in range(TT):
                stt(H[:, a, :], H[:, a, :], STAT[:, 3, a:a + 1], FG[:, :], ALU.mult, ALU.mult).then_inc(out_ready, 1)

        @block.tensor
        def _(pe):
            mm = nc.tensor.matmul
            pe.sem_inc(mm_done, CREDIT)
            pe.wait_ge(const_in, 32)

            def p1_quarter(g, p1g, q):
                t, kq = q // 4, q % 4
                if kq == 0:
                    pe.wait_ge(evac_done, p1g * 2 + t + 1)
                pe.wait_ge(lo_done, g * 8 + q + 1 + CREDIT)
                for j in range(4):
                    k = kq * 4 + j
                    whi, wlo = HI[:, kq, j * P:(j + 1) * P], LO[:, kq, j * P:(j + 1) * P]
                    mm(bank[t][:, 0:T], whi, Xhi[:, k, :], start=k == 0, stop=False)
                    mm(bank[t][:, 0:T], whi, Xlo[:, k, :], start=False, stop=False)
                    last = mm(bank[t][:, 0:T], wlo, Xhi[:, k, :], start=False, stop=k == KT - 1)
                last.then_inc(mm_done, 1)

            def p1_first(layer, phase, p1_base, number):
                def quarter(q):
                    p1_quarter(G(layer, phase, 0), layer * P1_LAYER + p1_base, q)

                for q in range(3):
                    transposes(number, *((0, 8), (8, 12), (12, KT))[q])
                    pe.wait_ge(xlo_done, number * KT + 4 * q + 4)
                    quarter(q)
                pe.wait_ge(xlo_done, number * KT + KT)
                for q in range(3, 8):
                    quarter(q)

            def p1(layer, phase, p1_base, first, end):
                with pe.Fori(first, end) as i:
                    for q in range(8):
                        p1_quarter(G(layer, phase, i), layer * P1_LAYER + p1_base + i, q)

            def p2_group(layer, phase, p2_base, i, start, stop):
                g = G(layer, phase, i)
                for q in range(8):
                    t, c = q // 4, q % 4
                    if c == 0:
                        pe.wait_ge(ylo_done, layer * (2 * P2_LAYER) + (i * 2 + (2 * p2_base + t + 1)))
                    pe.wait_ge(lo_done, g * 8 + q + 1 + CREDIT)
                    for a in range(TT):
                        yhi, ylo = Yhi[:, t, a * P:(a + 1) * P], Ylo[:, t, a * P:(a + 1) * P]
                        dst = bank[a * 4 + c][:, :]
                        mm(dst, yhi, HI[:, c, :], start=start and t == 0, stop=False)
                        mm(dst, yhi, LO[:, c, :], start=False, stop=False)
                        last = mm(dst, ylo, HI[:, c, :], start=False, stop=stop and t == 1)
                    last.then_inc(mm_done, 1)

            def p2(layer, phase, p2_base, n_groups):
                p2_group(layer, phase, p2_base, 0, True, False)
                with pe.Fori(1, n_groups - 1) as i:
                    p2_group(layer, phase, p2_base, i, False, False)
                p2_group(layer, phase, p2_base, n_groups - 1, False, True)

            def transposes(number, first, end):
                for k in range(first, end):
                    if k % 8 == 0:
                        pe.wait_ge(xn_dve, number * 2 + k // 8 + 1)
                        pe.wait_ge(xn_act, number * 2 + k // 8 + 1)
                    if k >= 6:
                        pe.wait_ge(xlo_done, number * KT + k - 6 + 1)
                    for a in range(TT):
                        last = nc.tensor.transpose(bank[2 + k % 6][:, a * P:(a + 1) * P],
                                                   XN[:, a, k * P:(k + 1) * P], IDENT[:, :])
                    last.then_inc(tr_done, 1)

            with pe.Fori(0, LAYERS) as layer:
                p1_first(layer, AT_IN, P1_IN, layer * 2)
                p1(layer, AT_IN, P1_IN, 1, 6)
                pe.wait_ge(pool_rows, layer + 1)
                for n in range(POOL_TILES):
                    last = mm(pool_out(n), flat(PW0, 2)[:, n * P:(n + 1) * P], W[:, LNY0 + n, :], start=True, stop=True)
                last.then_inc(pool_mm, 1)
                p1(layer, AT_IN, P1_IN, 6, G_IN)
                pe.wait_ge(conf_rows, layer * 6 + 6)
                for c in range(3):
                    mm(bank[2 + c][:, :], ONES[:, :], flat(C0 + 2 * c, 2), start=True, stop=True).then_inc(mean_mm, 1)
                for c in range(3):
                    pe.wait_ge(sq_done, layer * 3 + c + 1)
                    if c == 0:
                        pe.wait_ge(pool_used, layer + 1)
                    mm(bank[5 + c][:, :], ONES[:, :], flat(SQ0 + 2 * c, 2), start=True, stop=True).then_inc(var_mm, 1)
                p2(layer, AT_OUT, P2_OUT, G_OUT)
                p1_first(layer, AT_Q, P1_Q, layer * 2 + 1)
                stand(pe, keys_in, layer * 16 + 16)

                def scores(i):
                    pe.wait_ge(evac_done, layer * (2 * P1_LAYER) + (i * 2 + (2 * P1_Q + 2)))
                    pe.wait_ge(s_out, layer * HEADS + i)
                    for a in range(TT):
                        for j in range(2):
                            keys_of = KEY[:, bass.ds(i * 2 + (j - 2), 1), :].rearrange("p a n -> p (a n)")
                            last = mm(bank[2][:, (a * 2 + j) * KEYS:(a * 2 + j + 1) * KEYS],
                                      W[:, QT0 + j, a * P:(a + 1) * P], keys_of, start=True, stop=True)
                    last.then_inc(s_mm, 1)

                def q_group(phase, p1_base, i, head):
                    for q in range(8):
                        p1_quarter(G(layer, phase, i), layer * P1_LAYER + p1_base + i, q)
                        if q == 3 and head is not None:
                            scores(head)

                with pe.Fori(1, G_Q) as i:
                    q_group(AT_Q, P1_Q, i, i)
                q_group(AT_U, P1_U, 0, HEADS)
                p1(layer, AT_U, P1_U, 1, U_PICKS)
                pe.wait_ge(gates_done, layer + 1)
                for n in range(3):
                    for a in range(TT):
                        last = nc.tensor.transpose(bank[2 + n][:, a * P:(a + 1) * P], PK[:, n, a, :], IDENT[:, :])
                    last.then_inc(pt_mm, 1)
                p1(layer, AT_U, P1_U, U_PICKS, U_G0)

                with pe.Fori(0, G_U - U_G0) as n:
                    for q in range(8):
                        p1_quarter(G(layer, AT_U, n + U_G0), layer * P1_LAYER + (n + (P1_U + U_G0)), q)
                        if q % 4 == 1:
                            slot = q // 4
                            pe.wait_ge(hot_done, layer * (T // 4) + (n * 2 + (slot + 1)))
                            for j in range(4):
                                last = mm(bank[2 + slot][:, j * P:(j + 1) * P], OneA[:, j, :], OneB[:, j, :],
                                          start=True, stop=True)
                            last.then_inc(g_mm, 1)
                pe.wait_ge(evac_done, layer * (2 * P1_LAYER) + 2 * P1_LAYER + 2)
                p2(layer, AT_V, P2_V, G_V)


def _layout(inputs):
    f = {k: np.asarray(v) for k, v in inputs.items()}
    L = LAYERS

    def column_tiles(w):
        n = w.shape[2] // P
        return w.reshape(L, KT, P, n, P).transpose(0, 3, 2, 1, 4)

    win = column_tiles(f["w_in"])[:, WIN_ORDER]
    params = np.concatenate([
        f["norm1_g"].reshape(L, KT, P).transpose(0, 2, 1),
        f["norm2_g"].reshape(L, KT, P).transpose(0, 2, 1),
        f["pool_scale"].reshape(L, POOL_TILES, P).transpose(0, 2, 1),
        f["sconv_w"].reshape(L, SCONV_K * SCONV_TILES, P).transpose(0, 2, 1),
        f["conf_w"].reshape(L, CONF_K, CONF_TILES, P).transpose(0, 3, 2, 1).reshape(L, P, CONF_TILES * CONF_K),
        f["conf_b"].reshape(L, CONF_TILES, P).transpose(0, 2, 1),
        f["conf_ln_g"].reshape(L, CONF_TILES, P).transpose(0, 2, 1),
        f["conf_ln_b"].reshape(L, CONF_TILES, P).transpose(0, 2, 1),
    ], axis=2)
    keys = np.stack([f["peer_k1"], f["peer_k2"]], axis=2)
    u = f["peer_u"].reshape(L, KEYS, KEYS, KT, P).transpose(0, 2, 4, 3, 1)
    v = f["peer_v"].reshape(L, KEYS, KEYS, D).transpose(0, 2, 1, 3)
    count = np.minimum(np.arange(1, T + 1)[None, :], np.array(WINDOWS)[:, None])
    c = np.ascontiguousarray
    return {
        "x": c(f["x"].reshape(T, D)),
        "win": c(win).reshape(L * 2 * G_IN, P, D),
        "wout": c(f["w_out"]).reshape(L * 2 * G_OUT, P, D),
        "wq": c(column_tiles(f["peer_wq"])).reshape(L * 2 * G_Q, P, D),
        "ut": c(u).reshape(L * W_TILES, P, D),
        "vt": c(v).reshape(L * W_TILES, P, D),
        "params": c(params),
        "keys": c(keys.transpose(0, 4, 1, 2, 3).reshape(L, P, 2 * HEADS * KEYS)),
        "final_g": c(f["final_g"]),
        "iota": np.broadcast_to(np.arange(P, dtype=np.float32), (P, P)).copy(),
        "ident": np.eye(P, dtype=np.float32),
        "invcnt": np.broadcast_to((1.0 / count).astype(np.float32).reshape(1, -1), (P, POOL_TILES * T)).copy(),
        "poolw": c(f["pool_w"].transpose(0, 2, 1, 3).reshape(L, P, POOL_TILES * P)),
    }


def kernel(**inputs):
    import concourse.bacc as bacc
    from concourse.bass_utils import run_bass_kernel_spmd

    nc = bacc.Bacc("TRN2", target_bir_lowering=False, num_devices=1)
    arrays = _layout(inputs)
    args = [nc.dram_tensor(f"in_{n}", a.shape, F32, kind="ExternalInput").ap() for n, a in arrays.items()]
    out = nc.dram_tensor("out", (1, T, D), F32, kind="ExternalOutput").ap()
    build(nc, *args, out)
    result = run_bass_kernel_spmd(nc, [{f"in_{n}": a for n, a in arrays.items()}], core_ids=[0])
    return np.array(result.results[0]["out"])
```

```python
import numpy as np
import concourse.bass as bass
from concourse import mybir
from contextlib import ExitStack

F32 = mybir.dt.float32
F32R = mybir.dt.float32r
U32 = mybir.dt.uint32
ACT = mybir.ActivationFunctionType
ALU = mybir.AluOpType
AX = mybir.AxisListType

P = 128
T = 256
D = 2048
LAYERS = 2
TT = T // P
KT = D // P
POOL_TILES, SCONV_TILES, CONF_TILES = 4, 6, 6
SCONV_K, CONF_K = 3, 31
WINDOWS = (2, 4, 8, 16)
HEADS, TOPK, KEYS = 8, 16, 128
PICKS = HEADS * TOPK
EPS = 1e-6
NEG = -3.0e38

WIN_ORDER = ([n for i in range(6) for n in (22 + i, 28 + i)] + list(range(4))
             + list(range(4, 10)) + list(range(16, 22)) + list(range(10, 16)))

G_IN, G_OUT, G_Q, G_U, G_V = 17, 8, 8, 64, 64
AT_IN = 0
AT_OUT = AT_IN + G_IN
AT_Q = AT_OUT + G_OUT
AT_U = AT_Q + G_Q
AT_V = AT_U + G_U
G_LAYER = AT_V + G_V
P1_IN, P1_Q, P1_U, P1_LAYER = 0, G_IN, G_IN + G_Q, G_IN + G_Q + G_U
P2_OUT, P2_V, P2_LAYER = 0, G_OUT, G_OUT + G_V

C_G1, C_G2 = 0, 16
C_PS = 32
C_SW = C_PS + POOL_TILES
C_CW = C_SW + SCONV_K * SCONV_TILES
C_CB = C_CW + CONF_TILES * CONF_K
C_LG = C_CB + CONF_TILES
C_LB = C_LG + CONF_TILES
N_PAR = C_LB + CONF_TILES

W_TILES = 128
Y0 = 0
YS0 = Y0 + POOL_TILES
YC0 = YS0 + SCONV_TILES
HN0 = 16
DIAG0 = 10
FG0 = 0
ACC0, PACC0, PU0, PPROD0, PR0 = 16, 20, 24, 26, 26
Z0 = 32
ZP0 = Z0 + 2 * CONF_TILES
ZH0, ZGC0, ZGB0 = Z0 + 16, Z0 + 22, Z0 + 28
PPAD0, XPAD0, SA0, SB0 = 66, 73, 78, 83
U0, C0, XC0, SQ0, SACC0, INV0, LNY0, PW0 = 88, 92, 98, 104, 110, 116, 120, 126
JUNK0 = 98
CONF_DVE = 4
CONF_GROUPS = 3
G_CONV0 = 2
G_LN = G_CONV0 + CONF_DVE * CONF_GROUPS
LN_PACE = 5
TAP_SLOTS = (1, 4, 7, 9, 12, 15, 18, 20)
N_ACC = 4
KEY0, QT0, S0 = 0, 8, 112
PP, XP, UP = SCONV_K - 1 + T + 2, 16 + T, 32 + T

TOPK_Q = 3
TOPK_U = TT * HEADS - TOPK_Q
U_TOPK0 = 1
U_EXP = 28
U_PICKS = 31
U_G0 = 32
DIRECT = 2 * U_EXP
assert G_LN + 3 == G_IN
assert U_TOPK0 + 2 * TOPK_U < U_EXP and (G_U - U_G0) * 8 == T
WARM_START, WARM_NORM = 9, 20
CREDIT = 8


def build(nc, x, win, wout, wq, ut, vt, params, keys, final_g, iota, ident, invcnt, poolw, out):
    hs = nc.dram_tensor("h_saved_rows", (P, TT, D), F32, kind="Internal").ap()
    ctx = ExitStack()
    with ctx:
        cursor = [(nc.sbuf_base + 63) // 64 * 64]

        def region(nbytes):
            at = cursor[0]
            cursor[0] += (nbytes + 31) // 32 * 32
            return at

        def sb(name, shape, dt, at=None):
            nbytes = 4 * int(np.prod(shape[1:]))
            return nc.alloc_sbuf_tensor_at(name, shape, dt, offset=region(nbytes) if at is None else at)

        def sem(name):
            return ctx.enter_context(nc.semaphore(name))

        W = sb("W", [P, W_TILES, T], F32)
        at_xa, at_xb = region(16384), region(16384)
        Xhi = sb("Xhi", [P, KT, T], F32R, at_xa)
        Xlo = sb("Xlo", [P, KT, T], F32R, at_xb)
        H = sb("H", [P, TT, D], F32, at_xa)
        Yhi = sb("Yhi", [P, 2, T], F32R, at_xb)
        Ylo = sb("Ylo", [P, 2, T], F32R, at_xb + 2048)
        RAW = sb("RAW", [P, 4, 1024], F32)
        HI = sb("HI", [P, 4, 512], F32R)
        LO = sb("LO", [P, 4, 512], F32R)
        PAR = sb("PAR", [P, N_PAR], F32)
        IOTA = sb("IOTA", [P, P], F32)
        IDENT = sb("IDENT", [P, P], F32)
        ONES = sb("ONES", [P, P], F32)
        at_top = region(4096)
        CAND = sb("CAND", [P, 256], F32, at_top)
        CAND2 = sb("CAND2", [P, 256], F32, at_top + 1024)
        EQ1 = sb("EQ1", [P, TOPK, TOPK], F32, at_top + 2048)
        EQ2 = sb("EQ2", [P, TOPK, TOPK], F32, at_top + 3072)
        PT = sb("PT", [P, 3, T], F32, at_top)
        at_sc = region(2048)
        SC = sb("SC", [P, 2, KEYS], F32, at_sc)
        SC2 = sb("SC2", [P, 2, KEYS], F32, at_sc + 1024)
        GT = sb("GT", [P, 2, T], F32, at_sc)
        TV = sb("TV", [P, 2, TOPK], F32)
        TI = sb("TI", [P, 2, TOPK], U32)
        TIF = sb("TIF", [P, 2, TOPK], F32)
        BV = sb("BV", [P, TOPK], F32)
        BI = sb("BI", [P, TOPK], U32)
        BAB = sb("BAB", [P, 2, TOPK], U32)
        at_pk = region(4096)
        PK = sb("PK", [P, 3, TT, PICKS], F32, at_pk)
        OneA = sb("OneA", [P, 4, P], F32, at_pk)
        OneB = sb("OneB", [P, 4, P], F32, at_pk + 2048)
        SUMS = sb("SUMS", [P, TT * HEADS], F32)
        STAT = sb("STAT", [P, 8, TT], F32)
        SSQ = sb("SSQ", [P, TT, 4], F32)
        WC = sb("WC", [P, CONF_K + 1], F32)
        PS = sb("PS", [P, 3, 8], F32)
        assert cursor[0] <= nc.sbuf_usable_end, (cursor[0], nc.sbuf_usable_end)
        bank = [ctx.enter_context(nc.psum_tensor(f"bank{i}", [P, 512], F32)) for i in range(8)]

        def tiles(first, n):
            return W[:, first:first + n, :]

        def flat(first, n):
            return W[:, first:first + n, :].rearrange("p a t -> p (a t)")

        HN = flat(HN0, 16).rearrange("p (a d) -> p a d", a=TT)
        DIAG = W[:, DIAG0, :].rearrange("p (a n) -> p a n", a=TT)
        FG = flat(FG0, 8)
        PPAD = flat(PPAD0, 7)[:, 0:SCONV_TILES * PP].rearrange("p (a t) -> p a t", t=PP)
        XPAD = flat(XPAD0, 5)[:, 0:POOL_TILES * XP].rearrange("p (a t) -> p a t", t=XP)
        SA = flat(SA0, 5)[:, 0:POOL_TILES * XP].rearrange("p (a t) -> p a t", t=XP)
        SB = flat(SB0, 5)[:, 0:POOL_TILES * XP].rearrange("p (a t) -> p a t", t=XP)
        UPAD = flat(U0, 2)[:, 0:UP]
        PUPAD = flat(PU0, 2)[:, 0:UP]
        KEY = flat(KEY0, 8).rearrange("p (j n) -> p j n", n=KEYS)
        SBUFQ = flat(S0, 16).rearrange("p (a j n) -> p a j n", a=TT, n=KEYS)

        def pool_out(n):
            return bank[2 + n // 2][:, (n % 2) * T:(n % 2 + 1) * T]

        const_in = sem("const_in")
        x_in = [sem(f"x_in{c}") for c in range(4)]
        final_in = sem("final_in")
        par_in = sem("par_in")
        inv_in = sem("inv_in")
        keys_in = sem("keys_in")
        raw_in = [sem(f"raw_in{s}") for s in range(4)]
        hi_done = sem("hi_done")
        lo_done = sem("lo_done")
        mm_done = sem("mm_done")
        evac_done = sem("evac_done")
        yhi_done = sem("yhi_done")
        ylo_done = sem("ylo_done")
        h_ready = sem("h_ready")
        h_saved = sem("h_saved")
        h_back = sem("h_back")
        ssq_done = sem("ssq_done")
        var_done = sem("var_done")
        std_done = sem("std_done")
        rstd_done = sem("rstd_done")
        tr_done = sem("tr_done")
        xhi_done = sem("xhi_done")
        xlo_done = sem("xlo_done")
        pool_rows = sem("pool_rows")
        pool_mm = sem("pool_mm")
        pool_used = sem("pool_used")
        conf_rows = sem("conf_rows")
        conf_pool = sem("conf_pool")
        mean_mm = sem("mean_mm")
        cent_done = sem("cent_done")
        sq_done = sem("sq_done")
        var_mm = sem("var_mm")
        lstd_done = sem("lstd_done")
        lny_done = sem("lny_done")
        sig_done = sem("sig_done")
        sconv_out = sem("sconv_out")
        conf_out = sem("conf_out")
        s_mm = sem("s_mm")
        s_out = sem("s_out")
        topk_done = sem("topk_done")
        exp_done = sem("exp_done")
        gates_done = sem("gates_done")
        pt_mm = sem("pt_mm")
        hot_done = sem("hot_done")
        g_mm = sem("g_mm")
        g_used = sem("g_used")
        gated = sem("gated")
        ones_in = sem("ones_in")
        gm_done = sem("gm_done")
        passed = sem("passed")
        out_ready = sem("out_ready")
        out_done = sem("out_done")

        block = ctx.enter_context(nc.Block())

        def stand(eng, semaphore, value):
            eng.wait_ge(semaphore, value)
            eng.sem_inc(passed, 1)

        def G(layer, phase, i):
            return layer * G_LAYER + phase + i

        @block.sync
        def _(sp):
            def load(layer, src, per_layer, phase, n_groups):
                with sp.Fori(0, n_groups) as i:
                    for s in range(4):
                        sp.wait_ge(lo_done, G(layer, phase, i) * 8 + 2 * s + 2)
                        sp.dma_start(
                            RAW[:, s, :],
                            src[bass.ds(layer * per_layer + i * 2 + s // 2, 1), :,
                                (s % 2) * 1024:(s % 2 + 1) * 1024].rearrange("a p n -> p (a n)"),
                        ).then_inc(raw_in[s], 16)

            for c in range(4):
                sp.dma_start(HN[:, :, c * 512:(c + 1) * 512],
                             x.rearrange("(a p) d -> p a d", p=P)[:, :, c * 512:(c + 1) * 512]).then_inc(x_in[c], 16)
            with sp.Fori(0, LAYERS) as layer:
                load(layer, win, 2 * G_IN, AT_IN, G_IN)
                load(layer, wout, 2 * G_OUT, AT_OUT, G_OUT)
                load(layer, wq, 2 * G_Q, AT_Q, G_Q)
                load(layer, ut, 2 * G_U, AT_U, G_U)
                load(layer, vt, 2 * G_V, AT_V, G_V)
            for n in range(2 * TT):
                a, c = n // 2, n % 2
                sp.wait_ge(out_ready, n + 1)
                sp.dma_start(out[0, a * P:(a + 1) * P, c * 1024:(c + 1) * 1024],
                             HN[:, a, c * 1024:(c + 1) * 1024]).then_inc(out_done, 16)
            sp.wait_ge(out_done, 16 * 2 * TT)

        @block.gpsimd
        def _(pool):
            pool.dma_start(IDENT[:, :], ident).then_inc(const_in, 16)
            pool.dma_start(IOTA[:, :], iota).then_inc(const_in, 16)

            def save(norm):
                for c in range(4):
                    stand(pool, h_ready, norm * 8 + (2 * c + 2))
                    part = slice(c * 512, (c + 1) * 512)
                    pool.dma_start(hs[:, :, part], HN[:, :, part]).then_inc(h_saved, 16)

            def bring_back(norm, first_group):
                stand(pool, h_saved, norm * 64 + 64)
                for c in range(4):
                    stand(pool, mm_done, (first_group + c + 1) * 8 + CREDIT)
                    part = slice(c * 512, (c + 1) * 512)
                    pool.dma_start(H[:, :, part], hs[:, :, part]).then_inc(h_back, 16)

            def conformer_tiles(layer):
                stand(pool, par_in, layer * 16 + 16)
                stand(pool, tr_done, layer * (2 * KT) + KT)
                stand(pool, h_saved, layer * 128 + 64)
                nc.gpsimd.memset(PUPAD[:, 0:32], 0.0)
                for j in range(CONF_DVE, CONF_TILES):
                    stand(pool, evac_done, layer * (2 * P1_LAYER) + (2 * j + 2 + 2))
                    nc.gpsimd.tensor_tensor(PUPAD[:, 32:UP], W[:, Z0 + 2 * j, :], W[:, Z0 + 2 * j + 1, :], ALU.mult)
                    pool.drain()
                    for first in range(0, CONF_K, N_ACC):
                        n = min(N_ACC, CONF_K - first)
                        to = PACC0 if first == 0 else PPROD0
                        row = PUPAD[:, 2 + first:2 + first + T]
                        shifts = bass.AP(row.tensor, row.offset, [row.ap[0], [1, n], [1, T]])
                        at = C_CW + j * CONF_K + first
                        nc.gpsimd.tensor_tensor(tiles(to, n), shifts,
                                                PAR[:, at:at + n].unsqueeze(2).to_broadcast([P, n, T]), ALU.mult)
                        pool.drain()
                        if first > 0:
                            nc.gpsimd.tensor_tensor(tiles(PACC0, n), tiles(PACC0, n), tiles(to, n), ALU.add)
                            pool.drain()
                    nc.gpsimd.tensor_tensor(tiles(PACC0, 2), tiles(PACC0, 2), tiles(PACC0 + 2, 2), ALU.add)
                    pool.drain()
                    nc.gpsimd.tensor_tensor(W[:, PACC0, :], W[:, PACC0, :], W[:, PACC0 + 1, :], ALU.add)
                    pool.drain()
                    nc.gpsimd.tensor_tensor(W[:, C0 + j, :], W[:, PACC0, :],
                                            PAR[:, C_CB + j:C_CB + j + 1].to_broadcast([P, T]), ALU.add).then_inc(conf_pool, 1)

            def windows(layer):
                stand(pool, inv_in, layer * 32 + 32)
                nc.gpsimd.memset(XPAD[:, :, 0:16], 0.0)
                nc.gpsimd.memset(SA[:, :, 0:16], 0.0)
                nc.gpsimd.memset(SB[:, :, 0:16], 0.0)
                stand(pool, evac_done, layer * (2 * P1_LAYER) + (2 * CONF_TILES + POOL_TILES + 2))
                nc.gpsimd.tensor_copy(XPAD[:, :, 16:XP], tiles(ZP0, 4))
                pool.drain()
                steps = [(XPAD, SA, 0, 1), (SA, SB, 1, 2), (SB, SA, 2, 4), (SA, SB, 3, 8)]
                for src, dst, first, shift in steps:
                    nc.gpsimd.tensor_tensor(dst[:, first:4, 16:XP], src[:, first:4, 16:XP],
                                            src[:, first:4, 16 - shift:XP - shift], ALU.add)
                    pool.drain()
                    nc.gpsimd.tensor_tensor(W[:, PR0 + first, :], dst[:, first, 16:XP], W[:, INV0 + first, :], ALU.mult)
                pool.drain()
                nc.gpsimd.tensor_tensor(tiles(PR0, 4), tiles(PR0, 4), tiles(ZP0, 4), ALU.subtract).then_inc(pool_rows, 1)

            with pool.Fori(0, LAYERS) as layer:
                stand(pool, mm_done, layer * (G_LAYER * 8) + 1)
                pool.dma_start(PAR[:, :], params[bass.ds(layer, 1), :, :].rearrange("a p n -> p (a n)")).then_inc(par_in, 16)
                save(layer * 2)
                pool.dma_start(flat(INV0, 4), invcnt).then_inc(inv_in, 16)
                pool.dma_start(flat(PW0, 2), poolw[bass.ds(layer, 1), :, :].rearrange("a p n -> p (a n)")).then_inc(inv_in, 16)
                conformer_tiles(layer)
                windows(layer)
                bring_back(layer * 2, G(layer, AT_OUT, 0))
                save(layer * 2 + 1)
                pool.dma_start(flat(KEY0, 8), keys[bass.ds(layer, 1), :, :].rearrange("a p n -> p (a n)")).then_inc(keys_in, 16)
                stand(pool, rstd_done, layer * 2 + 2)
                nc.gpsimd.memset(flat(DIRECT, S0 - DIRECT), 1.0).then_inc(ones_in, 1)
                stand(pool, topk_done, layer + 1)
                nc.gpsimd.memset(flat(S0, W_TILES - S0), 1.0).then_inc(ones_in, 1)
                bring_back(layer * 2 + 1, G(layer, AT_V, 0))
            stand(pool, mm_done, (G(LAYERS - 1, AT_V, 0) + FG0 // 2 + 5) * 8 + CREDIT)
            pool.dma_start(FG[:, :], final_g.unsqueeze(0).to_broadcast([P, D])).then_inc(final_in, 16)

        @block.scalar
        def _(act):
            def hi(g, q):
                if q % 2 == 0:
                    act.wait_ge(raw_in[q // 2], g * 16 + 16)
                act.wait_ge(mm_done, g * 8 + q + 5)
                nc.scalar.activation(HI[:, q % 4, :], RAW[:, q // 2, (q % 2) * 512:(q % 2 + 1) * 512],
                                     ACT.Copy).then_inc(hi_done, 1)

            def evac(g, t, dst, func):
                act.wait_ge(mm_done, g * 8 + 4 * t + 4 + CREDIT)
                nc.scalar.activation(dst, bank[t][:, 0:T], func).then_inc(evac_done, 1)

            def p1_group(g, before, after, first=0):
                for q in range(first, 4):
                    hi(g, q)
                if before:
                    before()
                for q in range(4, 8):
                    hi(g, q)
                after()

            def wtile(n):
                return W[:, bass.ds(n, 1), :].rearrange("p a t -> p (a t)")

            def norm(number, gain, par_value, g_next):
                for c in range(4):
                    for a in range(TT):
                        act.wait_ge(h_ready, number * 8 + (2 * c + a + 1))
                        nc.scalar.activation(flat(JUNK0 + 2 * (a * 4 + c), 2), HN[:, a, c * 512:(c + 1) * 512],
                                             ACT.Square, accum_out=SSQ[:, a, c:c + 1]).then_inc(ssq_done, 1)
                act.wait_ge(var_done, number + 1)
                nc.scalar.activation(STAT[:, 2, :], STAT[:, 1, :], ACT.Sqrt).then_inc(std_done, 1)
                if gain is None:
                    return
                for q in range(3):
                    hi(g_next, q)
                act.wait_ge(par_in, par_value)
                for k in range(KT):
                    act.wait_ge(tr_done, number * KT + k + 1)
                    nc.scalar.activation(Xhi[:, k, :], bank[2 + k % 6][:, 0:T],
                                         ACT.Copy, scale=PAR[:, gain + k:gain + k + 1]).then_inc(xhi_done, 1)
                    if k == 11:
                        hi(g_next, 3)

            def y_hi(tile, t):
                nc.scalar.activation(Yhi[:, t, :], tile, ACT.Copy).then_inc(yhi_done, 1)

            def combine(layer, phase, n_groups, first_rows, last_evac, rows_ready, sides):
                g = G(layer, phase, 0)
                hi(g, 0)
                first_rows()
                act.wait_ge(mm_done, g * 8 - 3 + CREDIT)
                for t in range(2):
                    y_hi(W[:, t, :], t)
                for q in range(1, 4):
                    hi(g, q)
                last_evac()
                for q in range(4, 8):
                    hi(g, q)
                    if 0 in sides:
                        sides[0](q)

                def group(i, side):
                    g = G(layer, phase, i)
                    for t in range(2):
                        if rows_ready:
                            rows_ready(i, t)
                        act.wait_ge(mm_done, g * 8 + 4 * t + 4)
                        y_hi(wtile(i * 2 + t), t)
                        for q in range(4 * t, 4 * t + 4):
                            hi(g, q)
                            if side:
                                side(q)

                n_static = len(sides) or 1
                for i in range(1, n_static):
                    group(i, sides[i])
                act.preload_act_table(ACT.Sqrt)
                with act.Fori(n_static, n_groups) as i:
                    group(i, None)

            act.preload_act_table(ACT.Sqrt)
            with act.Fori(0, LAYERS) as layer:
                norm(layer * 2, C_G1, layer * 16 + 16, G(layer, AT_IN, 0))

                act.preload_act_table(ACT.Sigmoid)

                def z(i, t):
                    return wtile(i * 2 + (Z0 + t))

                def in_group(i, prev_func, first=0, between=None):
                    g = G(layer, AT_IN, i)

                    def before():
                        if prev_func is not None:
                            evac(g - 1, 1, z(i, -1), prev_func)
                        if between:
                            between()
                    p1_group(g, before, lambda: evac(g, 0, z(i, 0), ACT.Copy), first)

                in_group(0, None, 4)
                with act.Fori(1, CONF_TILES + 1) as i:
                    in_group(i, ACT.Sigmoid)
                with act.Fori(CONF_TILES + 1, G_LN + 1) as i:
                    in_group(i, ACT.Copy)

                def squares():
                    for c in range(3):
                        act.wait_ge(cent_done, layer * 3 + c + 1)
                        nc.scalar.activation(flat(SQ0 + 2 * c, 2), flat(XC0 + 2 * c, 2), ACT.Square).then_inc(sq_done, 1)
                    act.preload_act_table(ACT.Sqrt)

                in_group(G_LN + 1, ACT.Copy, 0, squares)

                def deviation(c):
                    act.wait_ge(var_mm, layer * 3 + c + 1)
                    nc.scalar.activation(flat(SQ0 + 2 * c, 2), bank[5 + c][:, :], ACT.Sqrt, bias=EPS).then_inc(lstd_done, 1)

                g_last = G(layer, AT_IN, G_IN - 1)
                for q in range(8):
                    hi(g_last, q)
                    if q == 3:
                        evac(g_last - 1, 1, W[:, Z0 + 2 * G_IN - 3, :], ACT.Copy)
                    if q >= 6:
                        deviation(q - 6)
                deviation(2)
                evac(g_last, 0, W[:, Z0 + 2 * G_IN - 2, :], ACT.Copy)

                def pool_rows_out():
                    act.wait_ge(pool_mm, layer + 1)
                    for n in range(POOL_TILES):
                        nc.scalar.activation(W[:, Y0 + n, :], pool_out(n), ACT.Copy,
                                             scale=PAR[:, C_PS + n:C_PS + n + 1]).then_inc(pool_used, 1)
                    act.wait_ge(pool_used, layer * POOL_TILES + POOL_TILES)

                def last_z():
                    evac(g_last, 1, W[:, Z0 + 2 * G_IN - 1, :], ACT.Copy)
                    act.preload_act_table(ACT.Sigmoid)

                def sigmoid(i):
                    def side(q):
                        slot = (i - 1) * 8 + q
                        if slot % LN_PACE == 3 and slot // LN_PACE < CONF_TILES:
                            n = slot // LN_PACE
                            act.wait_ge(lny_done, layer * CONF_TILES + n + 1)
                            nc.scalar.activation(W[:, XC0 + n, :], W[:, LNY0 + n, :], ACT.Sigmoid).then_inc(sig_done, 1)
                    return side

                def rows_ready(i, t):
                    if isinstance(i, int) and i * 2 < POOL_TILES:
                        return
                    if isinstance(i, int) and i * 2 < POOL_TILES + SCONV_TILES:
                        act.wait_ge(sconv_out, layer + 1)
                    else:
                        act.wait_ge(conf_out, layer * CONF_TILES + (i * 2 + (t + 1 - YC0)))

                combine(layer, AT_OUT, G_OUT, pool_rows_out, last_z, rows_ready,
                        {0: lambda q: None, **{i: sigmoid(i) for i in range(1, 5)}})
                norm(layer * 2 + 1, C_G2, layer * 16 + 16, G(layer, AT_Q, 0))

                act.preload_act_table(ACT.Gelu)

                def evac_q(i, t):
                    if t == 0:
                        act.wait_ge(s_mm, layer * HEADS + i)
                    evac(G(layer, AT_Q, i), t, W[:, QT0 + t, :], ACT.Copy)

                p1_group(G(layer, AT_Q, 0), None, lambda: evac(G(layer, AT_Q, 0), 0, W[:, QT0, :], ACT.Copy), 4)
                act.wait_ge(h_saved, layer * 128 + 128)
                with act.Fori(1, G_Q) as i:
                    p1_group(G(layer, AT_Q, i), lambda: evac_q(i - 1, 1), lambda: evac_q(i, 0))

                def u_evac(i, t, direct):
                    g = G(layer, AT_U, i)
                    if direct:
                        evac(g, t, wtile(i * 2 + t), ACT.Gelu)
                    else:
                        act.wait_ge(gm_done, layer * (W_TILES - DIRECT) + (i * 2 + (t + 1 - DIRECT)))
                        evac(g, t, GT[:, t, :], ACT.Gelu)

                def u_group(i, prev_direct, direct):
                    p1_group(G(layer, AT_U, i), lambda: u_evac(i - 1, 1, prev_direct), lambda: u_evac(i, 0, direct))

                p1_group(G(layer, AT_U, 0), lambda: evac_q(G_Q - 1, 1), lambda: u_evac(0, 0, True))
                with act.Fori(1, U_EXP) as i:
                    u_group(i, True, True)
                act.wait_ge(topk_done, layer + 1)
                gate_logits = PK[:, 0, :, :].rearrange("p a k -> p (a k)")
                nc.scalar.activation(gate_logits, gate_logits, ACT.Exp).then_inc(exp_done, 1)
                act.preload_act_table(ACT.Gelu)
                u_group(U_EXP, True, False)
                with act.Fori(U_EXP + 1, G_U) as i:
                    u_group(i, False, False)
                combine(layer, AT_V, G_V, lambda: act.wait_ge(gated, layer + 1),
                        lambda: u_evac(G_U - 1, 1, False), None, {})

            norm(2 * LAYERS, None, None, None)

        @block.vector
        def _(dve):
            tt = nc.vector.tensor_tensor
            ts = nc.vector.tensor_scalar
            stt = nc.vector.scalar_tensor_tensor

            def lo(g, q):
                dve.wait_ge(hi_done, g * 8 + q + 1)
                tt(LO[:, q % 4, :], RAW[:, q // 2, (q % 2) * 512:(q % 2 + 1) * 512],
                   HI[:, q % 4, :].bitcast(F32), ALU.subtract).then_inc(lo_done, 1)

            def lo_group(g, side=None, first=0):
                for q in range(first, 8):
                    lo(g, q)
                    if side:
                        side(q)

            def plain(layer, phase, first, end):
                with dve.Fori(first, end) as i:
                    lo_group(G(layer, phase, i))

            def norm(number, gain, par_value, g_next):
                dve.wait_ge(ssq_done, number * 8 + 8)
                nc.vector.tensor_reduce(STAT[:, 0, :], SSQ[:, :, :], AX.X, ALU.add)
                dve.drain()
                ts(STAT[:, 1, :], STAT[:, 0, :], 1.0 / D, EPS, ALU.mult, ALU.add).then_inc(var_done, 1)
                dve.wait_ge(std_done, number + 1)
                nc.vector.reciprocal(STAT[:, 3, :], STAT[:, 2, :])
                dve.drain()
                tt(STAT[:, 4, :], STAT[:, 3, :], STAT[:, 3, :], ALU.mult)
                dve.drain()
                stt(STAT[:, 5, :], STAT[:, 4, :], -0.5, STAT[:, 1, :], ALU.mult, ALU.mult)
                dve.drain()
                stt(STAT[:, 7, :], STAT[:, 5, :], 1.5, STAT[:, 3, :], ALU.add, ALU.mult)
                dve.drain()
                if gain is None:
                    return
                for a in range(TT):
                    last = ts(DIAG[:, a, :], IDENT[:, :], STAT[:, 7, a:a + 1], None, ALU.mult)
                last.then_inc(rstd_done, 1)
                lo(g_next, 0)
                lo(g_next, 1)
                dve.wait_ge(par_in, par_value)
                for k in range(KT):
                    dve.wait_ge(xhi_done, number * KT + k + 1)
                    stt(Xlo[:, k, :], bank[2 + k % 6][:, 0:T],
                        PAR[:, gain + k:gain + k + 1], Xhi[:, k, :].bitcast(F32),
                        ALU.mult, ALU.subtract).then_inc(xlo_done, 1)
                    if k in (7, 13):
                        lo(g_next, 2 if k == 7 else 3)

            def y_lo(layer, number, tile, t):
                dve.wait_ge(yhi_done, layer * (2 * P2_LAYER) + number)
                tt(Ylo[:, t, :], W[:, bass.ds(tile, 1), :].rearrange("p a t -> p (a t)"),
                   Yhi[:, t, :].bitcast(F32), ALU.subtract).then_inc(ylo_done, 1)

            def combine(layer, phase, p2_base, n_groups, back, between, sides):
                g = G(layer, phase, 0)
                lo(g, 0)
                for t in range(2):
                    y_lo(layer, 2 * p2_base + t + 1, t, t)
                for q in range(1, 4):
                    lo(g, q)
                between()
                for q in range(4, 8):
                    lo(g, q)

                def group(i, side):
                    for t in range(2):
                        y_lo(layer, i * 2 + (2 * p2_base + t + 1), i * 2 + t, t)
                        for q in range(4 * t, 4 * t + 4):
                            lo(G(layer, phase, i), q)
                            if side:
                                side(q)

                for n, side in enumerate(sides):
                    group(n + 1, side)
                with dve.Fori(1 + len(sides), n_groups) as i:
                    group(i, None)
                dve.wait_ge(h_back, back * 64 + 64)
                for c in range(4):
                    dve.wait_ge(mm_done, G(layer, phase, n_groups) * 8 + c - 3 + CREDIT)
                    for a in range(TT):
                        tt(HN[:, a, c * 512:(c + 1) * 512], bank[a * 4 + c][:, :],
                           H[:, a, c * 512:(c + 1) * 512], ALU.add).then_inc(h_ready, 1)

            dve.sem_inc(lo_done, CREDIT)
            dve.sem_inc(evac_done, 2)
            dve.sem_inc(gm_done, 2)
            dve.sem_inc(s_out, 1)
            nc.vector.memset(ONES[:, :], 1.0 / P)
            for c in range(4):
                dve.wait_ge(x_in[c], 16)
                dve.sem_inc(h_ready, TT)
            dve.wait_ge(const_in, 32)

            with dve.Fori(0, LAYERS) as layer:
                norm(layer * 2, C_G1, layer * 16 + 16, G(layer, AT_IN, 0))

                def z_done(n):
                    return layer * (2 * P1_LAYER) + n + 1 + 2

                nc.vector.memset(PPAD[:, :, 0:SCONV_K - 1], 0.0)
                nc.vector.memset(UPAD[:, 0:32], 0.0)
                lo_group(G(layer, AT_IN, 0), None, 4)
                plain(layer, AT_IN, 1, G_CONV0)
                stand(dve, h_saved, layer * 128 + 64)

                with dve.Fori(0, CONF_DVE) as j:
                    def taps(first):
                        for k in range(first, min(first + N_ACC, CONF_K)):
                            src, acc = UPAD[:, 2 + k:2 + k + T], W[:, ACC0 + k % N_ACC, :]
                            if k == 0:
                                ts(acc, src, WC[:, 0:1], WC[:, CONF_K:CONF_K + 1], ALU.mult, ALU.add)
                            elif k < N_ACC:
                                ts(acc, src, WC[:, k:k + 1], None, ALU.mult)
                            else:
                                stt(acc, src, WC[:, k:k + 1], acc, ALU.mult, ALU.add)
                        dve.drain()

                    def conv_side(n):
                        def side(q):
                            slot = n * 8 + q
                            if slot == 0:
                                dve.wait_ge(evac_done, layer * (2 * P1_LAYER) + (j * 2 + (2 + 2)))
                                pair = W[:, bass.ds(j * 2 + Z0, 2), :]
                                tt(UPAD[:, 32:UP], pair[:, 0, :], pair[:, 1, :], ALU.mult)
                                nc.vector.tensor_copy(WC[:, 0:CONF_K], PAR[:, bass.ds(j * CONF_K + C_CW, CONF_K)])
                                nc.vector.tensor_copy(WC[:, CONF_K:CONF_K + 1], PAR[:, bass.ds(j + C_CB, 1)])
                                dve.drain()
                            elif slot in TAP_SLOTS:
                                taps(TAP_SLOTS.index(slot) * N_ACC)
                            elif slot == CONF_GROUPS * 8 - 2:
                                tt(tiles(ACC0, 2), tiles(ACC0, 2), tiles(ACC0 + 2, 2), ALU.add)
                                dve.drain()
                            elif slot == CONF_GROUPS * 8 - 1:
                                tt(W[:, bass.ds(j + C0, 1), :].rearrange("p a t -> p (a t)"),
                                   W[:, ACC0, :], W[:, ACC0 + 1, :], ALU.add).then_inc(conf_rows, 1)
                                dve.drain()
                        return side

                    for n in range(CONF_GROUPS):
                        lo_group(G(layer, AT_IN, j * CONF_GROUPS + (G_CONV0 + n)), conv_side(n))

                def sconv_taps(n):
                    k = n // 2
                    for tile in range(n % 2 * 3, n % 2 * 3 + 3):
                        w = PAR[:, C_SW + k * SCONV_TILES + tile:C_SW + k * SCONV_TILES + tile + 1]
                        acc, src = W[:, SACC0 + tile, :], PPAD[:, tile, k:k + T]
                        if k == 0:
                            ts(acc, src, w, None, ALU.mult)
                        else:
                            stt(acc, src, w, acc, ALU.mult, ALU.add)
                    if n % 2:
                        dve.drain()

                def centred(c):
                    dve.wait_ge(mean_mm, layer * 3 + c + 1)
                    tt(flat(XC0 + 2 * c, 2), flat(C0 + 2 * c, 2), bank[2 + c][:, :], ALU.subtract).then_inc(cent_done, 1)

                def sconv_rows(first, end):
                    dve.wait_ge(evac_done, z_done(ZGB0 - Z0 + end - 1))
                    return tt(tiles(YS0 + first, end - first), tiles(SACC0 + first, end - first),
                              tiles(ZGB0 + first, end - first), ALU.mult)

                def ln_side(n):
                    def side(q):
                        slot = n * 8 + q
                        if slot == 5:
                            dve.wait_ge(evac_done, z_done(ZGB0 - Z0 - 1))
                            tt(PPAD[:, :, 2:2 + T], tiles(ZGC0, 6), tiles(ZH0, 6), ALU.mult)
                            dve.drain()
                        elif 8 <= slot < 11:
                            centred(slot - 8)
                        elif slot in (7, 11, 13, 15, 17, 19):
                            sconv_taps((7, 11, 13, 15, 17, 19).index(slot))
                        elif slot == 21:
                            sconv_rows(0, 4)
                    return side

                for n in range(3):
                    lo_group(G(layer, AT_IN, G_LN + n), ln_side(n))

                def rest_of_sconv():
                    sconv_rows(4, 6).then_inc(sconv_out, 1)

                def conformer_rows(i):
                    def side(q):
                        slot = (i - 1) * 8 + q
                        n, step = slot // LN_PACE, slot % LN_PACE
                        if n < CONF_TILES:
                            if step == 0:
                                dve.wait_ge(lstd_done, layer * 3 + n // 2 + 1)
                                nc.vector.reciprocal(W[:, C0 + n, :], W[:, SQ0 + n, :])
                                dve.drain()
                            elif step == 2:
                                tt(W[:, XC0 + n, :], W[:, XC0 + n, :], W[:, C0 + n, :], ALU.mult)
                                dve.drain()
                                ts(W[:, LNY0 + n, :], W[:, XC0 + n, :], PAR[:, C_LG + n:C_LG + n + 1],
                                   PAR[:, C_LB + n:C_LB + n + 1], ALU.mult, ALU.add).then_inc(lny_done, 1)
                        if step == 1 and 0 < n <= CONF_TILES:
                            dve.wait_ge(sig_done, layer * CONF_TILES + n)
                            tt(W[:, YC0 + n - 1, :], W[:, LNY0 + n - 1, :], W[:, XC0 + n - 1, :],
                               ALU.mult).then_inc(conf_out, 1)
                    return side

                combine(layer, AT_OUT, P2_OUT, G_OUT, layer * 2, rest_of_sconv,
                        [conformer_rows(i) for i in range(1, 5)])
                norm(layer * 2 + 1, C_G2, layer * 16 + 16, G(layer, AT_Q, 0))

                def scores_out(head, count):
                    dve.wait_ge(s_mm, count)
                    nc.vector.tensor_copy(SBUFQ[:, :, bass.ds(head * 2, 2), :],
                                          bank[2][:, :].rearrange("p (a j n) -> p a j n", a=TT, n=KEYS)
                                          ).then_inc(s_out, 1)

                def topk(b, group_a, group_b, end_a, end_b):
                    def half_topk(h):
                        first, second = slice(0, 8), slice(8, 16)
                        nc.vector.max(TV[:, h, first], SC[:, h, :])
                        dve.drain()
                        nc.vector.max_index(TI[:, h, first], TV[:, h, first], SC[:, h, :])
                        nc.vector.match_replace(SC2[:, h, :], TV[:, h, first], SC[:, h, :], NEG)
                        dve.drain()
                        nc.vector.max(TV[:, h, second], SC2[:, h, :])
                        dve.drain()
                        nc.vector.max_index(TI[:, h, second], TV[:, h, second], SC2[:, h, :])

                    def side_a(q):
                        if q == 0:
                            dve.drain()
                            nc.vector.tensor_copy(
                                SC[:, :, :],
                                flat(S0, 16)[:, bass.ds(b * (2 * KEYS), 2 * KEYS)].rearrange("p (j n) -> p j n", n=KEYS))
                            dve.drain()
                        elif q == 2:
                            half_topk(0)
                        elif q == 4:
                            half_topk(1)
                        elif q == 6:
                            dve.drain()
                            nc.vector.tensor_copy(TIF[:, :, :], TI[:, :, :])
                            tt(CAND[:, :].rearrange("p (a b) -> p a b", b=TOPK),
                               TV[:, 0, :].unsqueeze(2).to_broadcast([P, TOPK, TOPK]),
                               TV[:, 1, :].unsqueeze(1).to_broadcast([P, TOPK, TOPK]), ALU.add)
                            dve.drain()

                    def chosen(h, eq):
                        tt(eq[:, :, :], BAB[:, h, :].unsqueeze(2).to_broadcast([P, TOPK, TOPK]),
                           IOTA[:, 0:TOPK].unsqueeze(1).to_broadcast([P, TOPK, TOPK]), ALU.is_equal)

                    def times_keys(h, eq):
                        tt(eq[:, :, :], eq[:, :, :], TIF[:, h, :].unsqueeze(1).to_broadcast([P, TOPK, TOPK]), ALU.mult)

                    def summed(h, eq):
                        nc.vector.tensor_reduce(
                            PK[:, 1 + h, :, :].rearrange("p a k -> p (a k)")[:, bass.ds(b * TOPK, TOPK)],
                            eq[:, :, :], AX.X, ALU.add)

                    def side_b(q):
                        if q == 0:
                            nc.vector.max(BV[:, 0:8], CAND[:, :])
                            dve.drain()
                            nc.vector.max_index(BI[:, 0:8], BV[:, 0:8], CAND[:, :])
                            nc.vector.match_replace(CAND2[:, :], BV[:, 0:8], CAND[:, :], NEG)
                            dve.drain()
                        elif q == 1:
                            nc.vector.max(BV[:, 8:16], CAND2[:, :])
                            dve.drain()
                            nc.vector.max_index(BI[:, 8:16], BV[:, 8:16], CAND2[:, :])
                            dve.drain()
                        elif q == 2:
                            ts(BAB[:, 0, :], BI[:, :], 4, None, ALU.logical_shift_right)
                            ts(BAB[:, 1, :], BI[:, :], 15, None, ALU.bitwise_and)
                            ts(PK[:, 0, :, :].rearrange("p a k -> p (a k)")[:, bass.ds(b * TOPK, TOPK)],
                               BV[:, :], BV[:, 0:1], None, ALU.subtract)
                            dve.drain()
                        elif q == 3:
                            chosen(0, EQ1)
                            chosen(1, EQ2)
                            dve.drain()
                        elif q == 5:
                            times_keys(0, EQ1)
                            times_keys(1, EQ2)
                            dve.drain()
                        elif q == 6:
                            summed(0, EQ1)
                            summed(1, EQ2)
                            dve.drain()

                    lo_group(group_a, side_a)
                    end_a()
                    lo_group(group_b, side_b)
                    end_b()

                def nothing():
                    pass

                lo_group(G(layer, AT_Q, 0), None, 4)
                lo_group(G(layer, AT_Q, 1))
                scores_out(0, layer * HEADS + 1)
                with dve.Fori(0, TOPK_Q) as b:
                    topk(b, G(layer, AT_Q, b * 2 + 2), G(layer, AT_Q, b * 2 + 3),
                         lambda: scores_out(b * 2 + 1, layer * HEADS + (b * 2 + 2)),
                         lambda: scores_out(b * 2 + 2, layer * HEADS + (b * 2 + 3)))
                lo_group(G(layer, AT_U, 0))
                scores_out(HEADS - 1, layer * HEADS + HEADS)
                dve.drain()
                with dve.Fori(0, TOPK_U) as b:
                    topk(b + TOPK_Q, G(layer, AT_U, b * 2 + U_TOPK0), G(layer, AT_U, b * 2 + U_TOPK0 + 1),
                         nothing, nothing)
                dve.drain().then_inc(topk_done, 1)
                plain(layer, AT_U, U_TOPK0 + 2 * TOPK_U, U_EXP + 1)

                dve.wait_ge(exp_done, layer + 1)
                by_head = PK[:, 0, :, :].rearrange("p a (h k) -> p (a h) k", k=TOPK)
                nc.vector.tensor_reduce(SUMS[:, :], by_head, AX.X, ALU.add)
                dve.drain()
                nc.vector.reciprocal(SUMS[:, :], SUMS[:, :])
                dve.drain()
                tt(by_head, by_head, SUMS[:, :].unsqueeze(2).to_broadcast([P, TT * HEADS, TOPK]), ALU.mult).then_inc(gates_done, 1)

                def activation_in(i, t):
                    dve.wait_ge(evac_done, layer * (2 * P1_LAYER) + (i * 2 + (2 * P1_U + t + 3)))
                    rows = W[:, bass.ds(i * 2 + t, 1), :].rearrange("p a t -> p (a t)")
                    tt(rows, rows, GT[:, t, :], ALU.mult).then_inc(gm_done, 1)

                def activations_in(i):
                    def side(q):
                        if q in (2, 6):
                            activation_in(i - 1, q // 4)
                    return side

                def hot(slot):
                    tt(OneB[:, :, :], IOTA[:, :].unsqueeze(1).to_broadcast([P, 4, P]),
                       PS[:, 2, slot * 4:slot * 4 + 4].unsqueeze(2).to_broadcast([P, 4, P]), ALU.is_equal)
                    for c in range(slot * 4, slot * 4 + 4):
                        last = ts(OneA[:, c % 4, :], IOTA[:, :], PS[:, 1, c:c + 1], PS[:, 0, c:c + 1],
                                  ALU.is_equal, ALU.mult)
                    last.then_inc(hot_done, 1)

                def gate(token, four, slot, i):
                    dve.wait_ge(g_mm, four)
                    dve.wait_ge(gm_done, layer * (W_TILES - DIRECT) + i)
                    rows = W[:, :, bass.ds(token, 4)]
                    tt(rows, rows, bank[2 + slot][:, :].rearrange("p (t i) -> p i t", t=4), ALU.mult).then_inc(g_used, 1)

                def g_group(n, first):
                    i = n + U_G0
                    fours = layer * (T // 4) + n * 2

                    def side(q):
                        if q == 1:
                            if not first:
                                gate(n * 8 - 4, fours, 1, n * 2 + (2 * U_G0 - 2 - DIRECT + 2))
                            nc.vector.tensor_copy(PS[:, :, :], PT[:, :, bass.ds(n * 8, 8)])
                            dve.drain()
                            hot(0)
                        elif q == 2:
                            if not first:
                                dve.wait_ge(g_used, fours)
                            activation_in(i - 1, 0)
                        elif q == 5:
                            gate(n * 8, fours + 1, 0, n * 2 + (2 * U_G0 - 1 - DIRECT + 2))
                            hot(1)
                        elif q == 6:
                            dve.wait_ge(g_used, fours + 1)
                            activation_in(i - 1, 1)
                    lo_group(G(layer, AT_U, i), side)

                stand(dve, ones_in, layer * 2 + 2)
                with dve.Fori(U_EXP + 1, U_PICKS) as i:
                    lo_group(G(layer, AT_U, i), activations_in(i))

                def picks_in(q):
                    if q == 3:
                        for n in range(3):
                            dve.wait_ge(pt_mm, layer * 3 + n + 1)
                            nc.vector.tensor_copy(PT[:, n, :], bank[2 + n][:, 0:T])
                        dve.drain()
                    activations_in(U_PICKS)(q)
                lo_group(G(layer, AT_U, U_PICKS), picks_in)

                g_group(0, True)
                with dve.Fori(1, G_U - U_G0) as n:
                    g_group(n, False)
                gate(T - 4, layer * (T // 4) + T // 4, 1, 2 * (G_U - 1) - DIRECT + 2)
                dve.drain().then_inc(gated, 1)

                def last_activations():
                    activation_in(G_U - 1, 0)
                    activation_in(G_U - 1, 1)
                combine(layer, AT_V, P2_V, G_V, layer * 2 + 1, last_activations, [])

            norm(2 * LAYERS, None, None, None)
            dve.wait_ge(final_in, 16)
            for n in range(2 * TT):
                a, c = n // 2, n % 2
                part = HN[:, a, c * 1024:(c + 1) * 1024]
                stt(part, part, STAT[:, 7, a:a + 1], FG[:, c * 1024:(c + 1) * 1024], ALU.mult, ALU.mult).then_inc(out_ready, 1)

        @block.tensor
        def _(pe):
            mm = nc.tensor.matmul
            pe.sem_inc(mm_done, CREDIT)
            pe.wait_ge(const_in, 32)

            def keep_warm(n):
                for _ in range(n):
                    mm(bank[0][:, 0:P], IDENT[:, :], IDENT[:, :], start=True, stop=True)

            keep_warm(WARM_START)

            def p1_quarter(g, p1g, q):
                t, kq = q // 4, q % 4
                if kq == 0:
                    pe.wait_ge(evac_done, p1g * 2 + t + 1)
                pe.wait_ge(lo_done, g * 8 + q + 1 + CREDIT)
                for j in range(4):
                    k = kq * 4 + j
                    whi, wlo = HI[:, kq, j * P:(j + 1) * P], LO[:, kq, j * P:(j + 1) * P]
                    mm(bank[t][:, 0:T], whi, Xhi[:, k, :], start=k == 0, stop=False)
                    mm(bank[t][:, 0:T], whi, Xlo[:, k, :], start=False, stop=False)
                    last = mm(bank[t][:, 0:T], wlo, Xhi[:, k, :], start=False, stop=k == KT - 1)
                last.then_inc(mm_done, 1)

            def p1_first(layer, phase, p1_base, number):
                def quarter(q):
                    p1_quarter(G(layer, phase, 0), layer * P1_LAYER + p1_base, q)

                for q in range(3):
                    transposes(number, *((0, 8), (8, 12), (12, KT))[q])
                    pe.wait_ge(xlo_done, number * KT + 4 * q + 4)
                    quarter(q)
                pe.wait_ge(xlo_done, number * KT + KT)
                for q in range(3, 8):
                    quarter(q)

            def p1(layer, phase, p1_base, first, end):
                with pe.Fori(first, end) as i:
                    for q in range(8):
                        p1_quarter(G(layer, phase, i), layer * P1_LAYER + p1_base + i, q)

            def p2_group(layer, phase, p2_base, i, start, stop, bank_free=None):
                g = G(layer, phase, i)
                for q in range(8):
                    t, c = q // 4, q % 4
                    if c == 0:
                        pe.wait_ge(ylo_done, layer * (2 * P2_LAYER) + (i * 2 + (2 * p2_base + t + 1)))
                    pe.wait_ge(lo_done, g * 8 + q + 1 + CREDIT)
                    if bank_free and t == 0:
                        bank_free(c)
                    for a in range(TT):
                        yhi, ylo = Yhi[:, t, a * P:(a + 1) * P], Ylo[:, t, a * P:(a + 1) * P]
                        dst = bank[a * 4 + c][:, :]
                        mm(dst, yhi, HI[:, c, :], start=start and t == 0, stop=False)
                        mm(dst, yhi, LO[:, c, :], start=False, stop=False)
                        last = mm(dst, ylo, HI[:, c, :], start=False, stop=stop and t == 1)
                    last.then_inc(mm_done, 1)

            def p2(layer, phase, p2_base, n_groups, bank_free):
                p2_group(layer, phase, p2_base, 0, True, False, bank_free)
                with pe.Fori(1, n_groups - 1) as i:
                    p2_group(layer, phase, p2_base, i, False, False)
                p2_group(layer, phase, p2_base, n_groups - 1, False, True)

            def transposes(number, first, end):
                for k in range(first, end):
                    if k == 0:
                        pe.wait_ge(rstd_done, number + 1)
                    if k >= 6:
                        pe.wait_ge(xlo_done, number * KT + k - 6 + 1)
                    for a in range(TT):
                        last = mm(bank[2 + k % 6][:, a * P:(a + 1) * P],
                                  HN[:, a, k * P:(k + 1) * P], DIAG[:, a, :], start=True, stop=True)
                    last.then_inc(tr_done, 1)

            with pe.Fori(0, LAYERS) as layer:
                p1_first(layer, AT_IN, P1_IN, layer * 2)
                p1(layer, AT_IN, P1_IN, 1, G_LN)

                def sums(slot):
                    if slot == 3:
                        pe.wait_ge(conf_rows, layer * CONF_DVE + CONF_DVE)
                        pe.wait_ge(conf_pool, layer * (CONF_TILES - CONF_DVE) + (CONF_TILES - CONF_DVE))
                        for c in range(3):
                            mm(bank[2 + c][:, :], ONES[:, :], flat(C0 + 2 * c, 2), start=True, stop=True).then_inc(mean_mm, 1)
                    elif slot == 17:
                        for c in range(3):
                            pe.wait_ge(sq_done, layer * 3 + c + 1)
                            mm(bank[5 + c][:, :], ONES[:, :], flat(SQ0 + 2 * c, 2), start=True, stop=True).then_inc(var_mm, 1)
                    elif slot == 21:
                        pe.wait_ge(pool_rows, layer + 1)
                        pe.wait_ge(cent_done, layer * 3 + 3)
                        for n in range(POOL_TILES):
                            last = mm(pool_out(n), flat(PW0, 2)[:, n * P:(n + 1) * P], W[:, PR0 + n, :], start=True, stop=True)
                        last.then_inc(pool_mm, 1)

                for n in range(3):
                    for q in range(8):
                        p1_quarter(G(layer, AT_IN, G_LN + n), layer * P1_LAYER + P1_IN + G_LN + n, q)
                        sums(n * 8 + q)

                def out_bank_free(c):
                    if c == 0:
                        pe.wait_ge(evac_done, layer * (2 * P1_LAYER) + 2 * G_IN - 1 + 2)
                        pe.wait_ge(cent_done, layer * 3 + 3)
                    else:
                        pe.wait_ge(evac_done, layer * (2 * P1_LAYER) + 2 * G_IN + 2)
                        pe.wait_ge(lstd_done, layer * 3 + c)
                        pe.wait_ge(pool_used, layer * POOL_TILES + POOL_TILES)

                p2(layer, AT_OUT, P2_OUT, G_OUT, out_bank_free)
                stand(pe, h_ready, layer * 16 + 8 + 2)
                keep_warm(WARM_NORM)
                p1_first(layer, AT_Q, P1_Q, layer * 2 + 1)
                stand(pe, keys_in, layer * 16 + 16)

                def scores(i):
                    pe.wait_ge(evac_done, layer * (2 * P1_LAYER) + (i * 2 + (2 * P1_Q + 2)))
                    pe.wait_ge(s_out, layer * HEADS + i)
                    for a in range(TT):
                        for j in range(2):
                            keys_of = KEY[:, bass.ds(i * 2 + (j - 2), 1), :].rearrange("p a n -> p (a n)")
                            last = mm(bank[2][:, (a * 2 + j) * KEYS:(a * 2 + j + 1) * KEYS],
                                      W[:, QT0 + j, a * P:(a + 1) * P], keys_of, start=True, stop=True)
                    last.then_inc(s_mm, 1)

                def q_group(phase, p1_base, i, head):
                    for q in range(8):
                        p1_quarter(G(layer, phase, i), layer * P1_LAYER + p1_base + i, q)
                        if q == 3 and head is not None:
                            scores(head)

                with pe.Fori(1, G_Q) as i:
                    q_group(AT_Q, P1_Q, i, i)
                q_group(AT_U, P1_U, 0, HEADS)
                p1(layer, AT_U, P1_U, 1, U_PICKS)
                pe.wait_ge(gates_done, layer + 1)
                for n in range(3):
                    for a in range(TT):
                        last = nc.tensor.transpose(bank[2 + n][:, a * P:(a + 1) * P], PK[:, n, a, :], IDENT[:, :])
                    last.then_inc(pt_mm, 1)
                p1(layer, AT_U, P1_U, U_PICKS, U_G0)

                with pe.Fori(0, G_U - U_G0) as n:
                    for q in range(8):
                        p1_quarter(G(layer, AT_U, n + U_G0), layer * P1_LAYER + (n + (P1_U + U_G0)), q)
                        if q % 4 == 1:
                            slot = q // 4
                            pe.wait_ge(hot_done, layer * (T // 4) + (n * 2 + (slot + 1)))
                            for j in range(4):
                                last = mm(bank[2 + slot][:, j * P:(j + 1) * P], OneA[:, j, :], OneB[:, j, :],
                                          start=True, stop=True)
                            last.then_inc(g_mm, 1)

                def v_bank_free(c):
                    pe.wait_ge(evac_done, layer * (2 * P1_LAYER) + 2 * P1_LAYER + 2 - (c == 0))

                p2(layer, AT_V, P2_V, G_V, v_bank_free)
                stand(pe, h_ready, layer * 16 + 16 + 2)
                keep_warm(WARM_NORM)


def _layout(inputs):
    f = {k: np.asarray(v) for k, v in inputs.items()}
    L = LAYERS

    def column_tiles(w):
        n = w.shape[2] // P
        return w.reshape(L, KT, P, n, P).transpose(0, 3, 2, 1, 4)

    win = column_tiles(f["w_in"])[:, WIN_ORDER]
    params = np.concatenate([
        f["norm1_g"].reshape(L, KT, P).transpose(0, 2, 1),
        f["norm2_g"].reshape(L, KT, P).transpose(0, 2, 1),
        f["pool_scale"].reshape(L, POOL_TILES, P).transpose(0, 2, 1),
        f["sconv_w"].reshape(L, SCONV_K * SCONV_TILES, P).transpose(0, 2, 1),
        f["conf_w"].reshape(L, CONF_K, CONF_TILES, P).transpose(0, 3, 2, 1).reshape(L, P, CONF_TILES * CONF_K),
        f["conf_b"].reshape(L, CONF_TILES, P).transpose(0, 2, 1),
        f["conf_ln_g"].reshape(L, CONF_TILES, P).transpose(0, 2, 1),
        f["conf_ln_b"].reshape(L, CONF_TILES, P).transpose(0, 2, 1),
    ], axis=2)
    keys = np.stack([f["peer_k1"], f["peer_k2"]], axis=2)
    u = f["peer_u"].reshape(L, KEYS, KEYS, KT, P).transpose(0, 2, 4, 3, 1)
    v = f["peer_v"].reshape(L, KEYS, KEYS, D).transpose(0, 2, 1, 3)
    count = np.minimum(np.arange(1, T + 1)[None, :], np.array(WINDOWS)[:, None])
    c = np.ascontiguousarray
    return {
        "x": c(f["x"].reshape(T, D)),
        "win": c(win).reshape(L * 2 * G_IN, P, D),
        "wout": c(f["w_out"]).reshape(L * 2 * G_OUT, P, D),
        "wq": c(column_tiles(f["peer_wq"])).reshape(L * 2 * G_Q, P, D),
        "ut": c(u).reshape(L * W_TILES, P, D),
        "vt": c(v).reshape(L * W_TILES, P, D),
        "params": c(params),
        "keys": c(keys.transpose(0, 4, 1, 2, 3).reshape(L, P, 2 * HEADS * KEYS)),
        "final_g": c(f["final_g"]),
        "iota": np.broadcast_to(np.arange(P, dtype=np.float32), (P, P)).copy(),
        "ident": np.eye(P, dtype=np.float32),
        "invcnt": np.broadcast_to((1.0 / count).astype(np.float32).reshape(1, -1), (P, POOL_TILES * T)).copy(),
        "poolw": c(f["pool_w"].transpose(0, 2, 1, 3).reshape(L, P, POOL_TILES * P)),
    }


def kernel(**inputs):
    import concourse.bacc as bacc
    from concourse.bass_utils import run_bass_kernel_spmd

    nc = bacc.Bacc("TRN2", target_bir_lowering=False, num_devices=1)
    arrays = _layout(inputs)
    args = [nc.dram_tensor(f"in_{n}", a.shape, F32, kind="ExternalInput").ap() for n, a in arrays.items()]
    out = nc.dram_tensor("out", (1, T, D), F32, kind="ExternalOutput").ap()
    build(nc, *args, out)
    result = run_bass_kernel_spmd(nc, [{f"in_{n}": a for n, a in arrays.items()}], core_ids=[0])
    return np.array(result.results[0]["out"])
```
